# Optimizing a Trainium2 kernel written in Bass

```python
import jax, jax.numpy as jnp
from jax import lax
import numpy as np

D_MODEL = 1024
BATCH = 1
SEQ = 512
DEPTH = 2

Q_BLOCK = 128
SB_HEADS = 8
SB_HEAD_DIM = 64
MLA_HEADS = 8
MLA_NOPE_DIM = 64
MLA_ROPE_DIM = 32
MLA_V_DIM = 64
MLA_Q_RANK = 768
MLA_KV_RANK = 256
ROPE_THETA = 10000.0
CONV_WIDTH = D_MODEL
CONV_K = 3
D_FF = 2816
LN_EPS = 1e-5
RMS_EPS = 1e-6
DEEPNORM_ALPHA = (2 * DEPTH) ** 0.25
DEEPNORM_BETA = (8 * DEPTH) ** -0.25
N_EVEN = (DEPTH + 1) // 2
N_ODD = DEPTH // 2
SB_WIDTH = SB_HEADS * SB_HEAD_DIM
MLA_WIDTH = MLA_HEADS * MLA_V_DIM
MIX_IN_SPLITS = (SB_WIDTH, 2 * SB_WIDTH, 3 * SB_WIDTH,
                 3 * SB_WIDTH + MLA_Q_RANK, 3 * SB_WIDTH + MLA_Q_RANK + MLA_KV_RANK)
MIX_IN_WIDTH = 3 * SB_WIDTH + MLA_Q_RANK + MLA_KV_RANK + MLA_ROPE_DIM

kernel_name = "hybrid_stickbreak_mla_shortconv_macaron"

def layer_norm(x, g, b):
    xf = x.astype(jnp.float32)
    mu = jnp.mean(xf, -1, keepdims=True)
    var = jnp.mean(jnp.square(xf - mu), -1, keepdims=True)
    y = (xf - mu) * lax.rsqrt(var + LN_EPS) * g.astype(jnp.float32) + b.astype(jnp.float32)
    return y.astype(x.dtype)

def rms_norm(x, g):
    xf = x.astype(jnp.float32)
    y = xf * lax.rsqrt(jnp.mean(xf * xf, -1, keepdims=True) + RMS_EPS) * g.astype(jnp.float32)
    return y.astype(x.dtype)

def swiglu(x, w_gate, w_up, w_down):
    return (jax.nn.silu(x @ w_gate) * (x @ w_up)) @ w_down

def rope_tables(seq, dtype):
    inv_freq = ROPE_THETA ** (-jnp.arange(0, MLA_ROPE_DIM, 2, dtype=jnp.float32) / MLA_ROPE_DIM)
    ang = jnp.arange(seq, dtype=jnp.float32)[:, None] * inv_freq[None, :]
    return jnp.cos(ang).astype(dtype), jnp.sin(ang).astype(dtype)

def apply_rope(x, cos, sin):
    half = x.shape[-1] // 2
    x1, x2 = x[..., :half], x[..., half:]
    return jnp.concatenate([x1 * cos - x2 * sin, x2 * cos + x1 * sin], axis=-1)

def to_blocks(t):
    b, s = t.shape[:2]
    return t.reshape(b, s // Q_BLOCK, Q_BLOCK, *t.shape[2:]).swapaxes(0, 1)

def from_blocks(t):
    nb, b, qb = t.shape[:3]
    return t.swapaxes(0, 1).reshape(b, nb * qb, *t.shape[3:])

def stick_breaking_attention(q, k, v):
    seq, d = q.shape[1], q.shape[-1]
    scale = d ** -0.5
    key_pos = jnp.arange(seq)

    def one_block(args):
        qb, blk = args
        q_pos = blk * Q_BLOCK + jnp.arange(Q_BLOCK)
        z = jnp.einsum('bqhd,bkhd->bhqk', qb, k, preferred_element_type=jnp.float32) * scale
        past = key_pos[None, :] < q_pos[:, None]
        log_beta = jax.nn.log_sigmoid(z)
        log_not = jnp.where(past, log_beta - z, 0.0)
        later = lax.cumsum(log_not, axis=3, reverse=True) - log_not
        w = jnp.where(past, jnp.exp(log_beta + later), 0.0)
        return jnp.einsum('bhqk,bkhd->bqhd', w.astype(v.dtype), v)

    out = lax.map(one_block, (to_blocks(q), jnp.arange(seq // Q_BLOCK)))
    return from_blocks(out)

def mla_attention(q_nope, q_rope, k_nope, k_rope, v):
    seq = q_nope.shape[1]
    scale = (MLA_NOPE_DIM + MLA_ROPE_DIM) ** -0.5
    key_pos = jnp.arange(seq)

    def one_block(args):
        qn, qr, blk = args
        q_pos = blk * Q_BLOCK + jnp.arange(Q_BLOCK)
        s = (jnp.einsum('bqhd,bkhd->bhqk', qn, k_nope, preferred_element_type=jnp.float32)
             + jnp.einsum('bqhr,bkr->bhqk', qr, k_rope, preferred_element_type=jnp.float32)) * scale
        s = jnp.where(key_pos[None, :] <= q_pos[:, None], s, -jnp.inf)
        p = jax.nn.softmax(s, axis=-1)
        return jnp.einsum('bhqk,bkhd->bqhd', p.astype(v.dtype), v)

    out = lax.map(one_block, (to_blocks(q_nope), to_blocks(q_rope), jnp.arange(seq // Q_BLOCK)))
    return from_blocks(out)

def attention_group_mixer(x, w_in, q_norm_g, w_uq, kv_norm_g, w_ukv, w_out, cos, sin):
    b, s, _ = x.shape
    q_sb, k_sb, v_sb, c_q, c_kv, k_rope = jnp.split(x @ w_in, MIX_IN_SPLITS, axis=-1)
    sb_shape = (b, s, SB_HEADS, SB_HEAD_DIM)
    out_sb = stick_breaking_attention(q_sb.reshape(sb_shape), k_sb.reshape(sb_shape),
                                      v_sb.reshape(sb_shape)).reshape(b, s, SB_WIDTH)
    q = (rms_norm(c_q, q_norm_g) @ w_uq).reshape(b, s, MLA_HEADS, MLA_NOPE_DIM + MLA_ROPE_DIM)
    q_nope = q[..., :MLA_NOPE_DIM]
    q_rope = apply_rope(q[..., MLA_NOPE_DIM:], cos[:, None, :], sin[:, None, :])
    kv = (rms_norm(c_kv, kv_norm_g) @ w_ukv).reshape(b, s, MLA_HEADS, MLA_NOPE_DIM + MLA_V_DIM)
    k_nope, v = kv[..., :MLA_NOPE_DIM], kv[..., MLA_NOPE_DIM:]
    k_rope = apply_rope(k_rope, cos, sin)
    out_mla = mla_attention(q_nope, q_rope, k_nope, k_rope, v).reshape(b, s, MLA_WIDTH)
    return jnp.concatenate([out_sb, out_mla], axis=-1) @ w_out

def short_conv_mixer(x, w_in, conv_w, w_out):
    gate_b, gate_c, h = jnp.split(x @ w_in, 3, axis=-1)
    u = gate_c * h
    conv = lax.conv_general_dilated(
        u, conv_w[:, None, :], window_strides=(1,), padding=[(CONV_K - 1, 0)],
        dimension_numbers=('NWC', 'WIO', 'NWC'), feature_group_count=CONV_WIDTH)
    return (gate_b * conv) @ w_out

def _dense(key, shape, fan_in, scale=1.0):
    return jax.random.normal(key, shape, jnp.float32) * (scale * fan_in ** -0.5)

def setup_inputs(seed: int = 0) -> dict:
    key = jax.random.key(seed)
    ks = jax.random.split(key, 16)
    n = lambda k, shape: jax.random.normal(k, shape, jnp.float32)
    mix_out_in = SB_WIDTH + MLA_WIDTH
    return {
        "x": n(ks[0], (BATCH, SEQ, D_MODEL)),
        "ln_g": 1.0 + 0.02 * n(ks[1], (DEPTH, 3, D_MODEL)),
        "ln_b": 0.02 * n(ks[2], (DEPTH, 3, D_MODEL)),
        "ffn_w_gate": _dense(ks[3], (DEPTH, 2, D_MODEL, D_FF), D_MODEL),
        "ffn_w_up": _dense(ks[4], (DEPTH, 2, D_MODEL, D_FF), D_MODEL),
        "ffn_w_down": _dense(ks[5], (DEPTH, 2, D_FF, D_MODEL), D_FF, DEEPNORM_BETA),
        "mix_w_in": _dense(ks[6], (N_EVEN, D_MODEL, MIX_IN_WIDTH), D_MODEL),
        "mla_q_norm_g": 1.0 + 0.02 * n(ks[7], (N_EVEN, MLA_Q_RANK)),
        "mla_w_uq": _dense(ks[8], (N_EVEN, MLA_Q_RANK, MLA_HEADS * (MLA_NOPE_DIM + MLA_ROPE_DIM)), MLA_Q_RANK),
        "mla_kv_norm_g": 1.0 + 0.02 * n(ks[9], (N_EVEN, MLA_KV_RANK)),
        "mla_w_ukv": _dense(ks[10], (N_EVEN, MLA_KV_RANK, MLA_HEADS * (MLA_NOPE_DIM + MLA_V_DIM)), MLA_KV_RANK),
        "mix_w_out": _dense(ks[11], (N_EVEN, mix_out_in, D_MODEL), mix_out_in, DEEPNORM_BETA),
        "conv_w_in": _dense(ks[12], (N_ODD, D_MODEL, 3 * CONV_WIDTH), D_MODEL),
        "conv_w": _dense(ks[13], (N_ODD, CONV_K, CONV_WIDTH), CONV_K),
        "conv_w_out": _dense(ks[14], (N_ODD, CONV_WIDTH, D_MODEL), CONV_WIDTH, DEEPNORM_BETA),
    }

def reference(x, ln_g, ln_b, ffn_w_gate, ffn_w_up, ffn_w_down, mix_w_in, mla_q_norm_g, mla_w_uq,
              mla_kv_norm_g, mla_w_ukv, mix_w_out, conv_w_in, conv_w, conv_w_out):
    cos, sin = rope_tables(x.shape[1], x.dtype)
    for layer in range(DEPTH):
        j = layer // 2
        f1 = swiglu(x, ffn_w_gate[layer, 0], ffn_w_up[layer, 0], ffn_w_down[layer, 0])
        x = layer_norm(DEEPNORM_ALPHA * x + 0.5 * f1, ln_g[layer, 0], ln_b[layer, 0])
        if layer % 2 == 0:
            m = attention_group_mixer(x, mix_w_in[j], mla_q_norm_g[j], mla_w_uq[j], mla_kv_norm_g[j],
                                      mla_w_ukv[j], mix_w_out[j], cos, sin)
        else:
            m = short_conv_mixer(x, conv_w_in[j], conv_w[j], conv_w_out[j])
        x = layer_norm(DEEPNORM_ALPHA * x + m, ln_g[layer, 1], ln_b[layer, 1])
        f2 = swiglu(x, ffn_w_gate[layer, 1], ffn_w_up[layer, 1], ffn_w_down[layer, 1])
        x = layer_norm(DEEPNORM_ALPHA * x + 0.5 * f2, ln_g[layer, 2], ln_b[layer, 2])
    return x


_drawn_inputs = setup_inputs


def setup_inputs(seed=0):
    import zlib

    import numpy as np

    out = dict(_drawn_inputs(seed))
    spreads = {}
    factors = {'mla_q_norm_g': 8.0, 'mla_kv_norm_g': 8.0}
    for name, (base, spread) in spreads.items():
        noise = np.random.default_rng([zlib.crc32(name.encode()), seed]).standard_normal(out[name].shape)
        drawn = base * np.exp(spread * noise) if base else spread * noise
        out[name] = __import__('jax').numpy.asarray(drawn.astype(out[name].dtype))
    for name, factor in factors.items():
        out[name] = (out[name] * factor).astype(out[name].dtype)
    return out
```

```python
from contextlib import ExitStack

import numpy as np

import concourse.bass as bass
from concourse import mybir

F32 = mybir.dt.float32
F32R = mybir.dt.float32r
ALU = mybir.AluOpType
ACT = mybir.ActivationFunctionType
AX = mybir.AxisListType

P = 128
S = 512
D = 1024
F = 2816
KT = D // P
TT = S // P
FT = F // P
PAIRS = FT // 2
UNIT = KT * 2 * P
HALF = D // 2
ALPHA = 4.0 ** 0.25
LN_EPS = 1e-5
RMS_EPS = 1e-6

SB_W = 512
HD = 64
ROPE = 32
Q_RANK = 768
KV_RANK = 256
MLA_HEAD_Q = HD + ROPE
MLA_SCALE = float(MLA_HEAD_Q) ** -0.5
HEAD_PAIRS = 4
LATENT_UNITS = (Q_RANK + KV_RANK) // 256
OUT_UNITS = D // 256
DOWN_UNITS = F // 256
FFN_TAIL = (2, 0, 1)
MIX_TAIL = (1, 2, 0)

STAGES = (("ffn", 0, 0), ("attn", 0, 1), ("ffn", 0, 2), ("ffn", 1, 0), ("conv", 1, 1), ("ffn", 1, 2))

SLOT_UNITS = {"ffn": (16, 16, 1), "conv": (6, 5, 5), "attn": (12, 11, 2)}
SLOT_DMAS = {"ffn": (16, 16, 1), "conv": (6, 5, 5), "attn": (16, 11, 2)}
LEFT_UNITS = {"ffn": (5, 5, 1), "conv": (2, 1, 1), "attn": (2, 1, 1)}
DOWN_USED = {"ffn": 10, "conv": 3, "attn": 3}

C_IDENT, C_NEG_ONES, C_NEG_TRI, C_PAST, C_NOT_PAST, C_CAUSAL, C_COLS = 0, 128, 256, 384, 512, 640, 768
ROWS_TAPS, ROWS_QG, ROWS_KVG, N_ROWS = 0, 24, 30, 32


def build_trunk(nc, x, ln_g, ln_b, w_gate, w_up, w_down, mix_in, q_norm_g, w_uq, kv_norm_g, w_ukv,
                mix_out, conv_in, conv_w, conv_out, consts, rope, out, stages=STAGES):
    n_stages = len(stages)

    def before(table, k, s=None):
        return sum(table[kind][s] if s is not None else table[kind] for kind, _, _ in stages[:k])

    def ffns_before(k):
        return sum(kind == "ffn" for kind, _, _ in stages[:k])

    with ExitStack() as ctx:
        def sb(name, shape, dt):
            return ctx.enter_context(nc.sbuf_tensor(name, shape, dt))

        def sem(name):
            return ctx.enter_context(nc.semaphore(name))

        raw = [sb(f"raw{s}", [P, UNIT], F32) for s in range(3)]
        w_hi = [sb(f"w_hi{s}", [P, UNIT], F32R) for s in range(3)]
        w_lo = [sb(f"w_lo{s}", [P, UNIT], F32R) for s in range(3)]
        left_hi = [sb(f"left_hi{s}", [P, 2, S], F32R) for s in range(3)]
        left_lo = [sb(f"left_lo{s}", [P, 2, S], F32R) for s in range(3)]
        xn = sb("xn", [P, TT, D], F32)
        xT_hi = sb("xT_hi", [P, KT, S], F32R)
        xT_lo = sb("xT_lo", [P, KT, S], F32R)
        h = sb("h", [P, FT, S], F32)
        gb = sb("gb", [P, 2, D], F32)
        gs = sb("gs", [P, 2, S], F32)
        cst = sb("cst", [P, C_COLS], F32)
        rows = sb("rows", [N_ROWS, P], F32)
        cols = sb("cols", [P, N_ROWS], F32)
        stats = sb("stats", [P, 2, 6], F32)
        mean_var = sb("mean_var", [P, 2], F32)
        neg_max = sb("neg_max", [P, TT], F32)
        p_sum = sb("p_sum", [P, TT], F32)
        veps = sb("veps", [P, 1], F32)
        rstd = sb("rstd", [P, TT], F32)
        half_neg = sb("half_neg", [P, 1], F32)
        taps = sb("taps", [P, 3, 2], F32)
        rope_sb = sb("rope_sb", [P, S], F32)
        ident_r = sb("ident_r", [P, P], F32R)
        not_past_r = sb("not_past_r", [P, P], F32R)
        ps = ctx.enter_context(nc.psum_tensor("ps", [P, 8, 512], F32))

        ident = cst[:, C_IDENT:C_IDENT + P]

        x_in = [sem(f"x_in{t}") for t in range(TT)]
        ident_in = sem("ident_in")
        consts_in = sem("consts_in")
        raw_full = [sem(f"raw_full{s}") for s in range(3)]
        gb_full = sem("gb_full")
        out_stored = sem("out_stored")
        w_hi_done = [sem(f"w_hi_done{s}") for s in range(3)]
        w_lo_done = [sem(f"w_lo_done{s}") for s in range(3)]
        left_hi_done = [sem(f"left_hi_done{s}") for s in range(3)]
        left_lo_done = [sem(f"left_lo_done{s}") for s in range(3)]
        down_used = sem("down_used")
        gate_done = sem("gate_done")
        up_done = sem("up_done")
        silu_done = sem("silu_done")
        h_done = sem("h_done")
        conv_c_done = sem("conv_c_done")
        conv_h_done = sem("conv_h_done")
        conv_b_done = sem("conv_b_done")
        c_copied = sem("c_copied")
        u_done = sem("u_done")
        conv_step = sem("conv_step")
        conv_out_done = sem("conv_out_done")
        u_zeroed = sem("u_zeroed")
        taps_set = sem("taps_set")
        lat_done = sem("lat_done")
        lat_squared = sem("lat_squared")
        sums_zeroed = sem("sums_zeroed")
        sq_added = sem("sq_added")
        sum_done = sem("sum_done")
        rms_ready = sem("rms_ready")
        lat_scaled = sem("lat_scaled")
        lat_hi_done = sem("lat_hi_done")
        lat_ready = sem("lat_ready")
        kr_done = sem("kr_done")
        kr_step = sem("kr_step")
        masks_ready = sem("masks_ready")
        sbq_done = sem("sbq_done")
        sbk_done = sem("sbk_done")
        sbv_done = sem("sbv_done")
        sbq_hi_done = sem("sbq_hi_done")
        sbk_hi_done = sem("sbk_hi_done")
        sbq_ready = sem("sbq_ready")
        sbk_ready = sem("sbk_ready")
        sb_vT_copied = sem("sb_vT_copied")
        sb_v_turned = sem("sb_v_turned")
        sb_v_ready = sem("sb_v_ready")
        z_done = sem("z_done")
        soft_step = sem("soft_step")
        log_ready = sem("log_ready")
        keep_step = sem("keep_step")
        keep_ready = sem("keep_ready")
        stick_done = sem("stick_done")
        sb_w_done = sem("sb_w_done")
        sb_pv_done = sem("sb_pv_done")
        sb_oA_copied = sem("sb_oA_copied")
        sb_oB_copied = sem("sb_oB_copied")
        mq_done = sem("mq_done")
        mk_done = sem("mk_done")
        mv_done = sem("mv_done")
        mq_step = sem("mq_step")
        mq_nope_copied = sem("mq_nope_copied")
        mq_rope_ready = sem("mq_rope_ready")
        mk_copied = sem("mk_copied")
        k_rope_placed = sem("k_rope_placed")
        mvT_copied = sem("mvT_copied")
        mv_turned = sem("mv_turned")
        mv_ready = sem("mv_ready")
        s_done = sem("s_done")
        max_step = sem("max_step")
        max_ready = sem("max_ready")
        exp_done = sem("exp_done")
        norm_step = sem("norm_step")
        p_ready = sem("p_ready")
        p_turned = sem("p_turned")
        pT_copied = sem("pT_copied")
        mla_pv_done = sem("mla_pv_done")
        mla_oA_copied = sem("mla_oA_copied")
        mla_oB_copied = sem("mla_oB_copied")
        y_done = sem("y_done")
        ln_step = sem("ln_step")
        var_ready = sem("var_ready")
        rstd_ready = sem("rstd_ready")
        rms_step = sem("rms_step")
        x_done = sem("x_done")
        turned = sem("turned")
        xT_hi_done = sem("xT_hi_done")
        xT_ready = sem("xT_ready")
        res_ready = sem("res_ready")
        rows_turned = sem("rows_turned")
        cols_ready = sem("cols_ready")
        exp_ready = sem("exp_ready")

        h_flat = h[:].rearrange("p f s -> p (f s)")
        U_PAD = 2
        U_W = S + 4
        conv_u = [h_flat[:, KT * S + c * U_W:KT * S + (c + 1) * U_W] for c in range(2)]
        conv_acc = [h[:, KT + 4 + c, :] for c in range(2)]

        latent = [h[:, KT + ct, :] for ct in range(KT)]
        pT = [h[:, KT + 4 * a:KT + 4 * a + 4, :] for a in range(2)]
        scratch = [raw[2][:, n * S:(n + 1) * S] for n in range(4)]
        k_rope, sq_sum, rope_tmp, mla_vT = scratch[0], scratch[1:3], scratch[3], scratch[0]
        sbq = (left_hi[0][:, 0, :], left_lo[0][:, 0, :])
        sbk = (left_hi[0][:, 1, :], left_lo[0][:, 1, :])
        sb_vT, sb_v = gs[:, 0, :], gs[:, 1, :].rearrange("p (k n) -> p k n", k=TT)
        Z_W = sum(S - P * i for i in range(TT))
        Z_AT = (0, 512, 1024, 896)
        stick = [h_flat[:, 2 * KT * S + a * Z_W:2 * KT * S + (a + 1) * Z_W] for a in range(2)]
        ps_flat = ps[:].rearrange("p b n -> p (b n)")
        z = [ps_flat[:, 1536 * a:1536 * a + Z_W] for a in range(2)]
        mq = [gs[:, a, :] for a in range(2)]
        mk = [h[:, 19 + a, :] for a in range(2)]
        mv = h[:, 21, :].rearrange("p (k n) -> p k n", k=TT)
        prob = [h[:, 16, :], h[:, 17, :], h[:, 18, :], scratch[1]]

        def kv_view(w, part):
            return w[:, 0:2 * 256].rearrange("p (k c a n) -> p k c a n", k=2, c=2, a=2)[:, :, part, :, :]

        def kv_raw(part):
            return raw[1][:, 0:2 * 256].rearrange("p (k a c n) -> p k a c n", k=2, a=2, c=2)[:, :, :, part, :]

        LAT_BANK = (0, 1, 2, 3, 5, 6, 7, 0)
        up_view = [(w_hi[s][:].rearrange("p (k n) -> p k n", k=KT), w_lo[s][:].rearrange("p (k n) -> p k n", k=KT))
                   for s in range(3)]
        down_view = [(w_hi[s][:].rearrange("p (f n) -> p f n", f=2), w_lo[s][:].rearrange("p (f n) -> p f n", f=2))
                     for s in range(3)]

        def col_units(w, col):
            return w.rearrange("(k p) n -> p k n", p=P)[:, :, bass.ds(col, 256)]

        def row_units(w, u):
            return w[bass.ds(u * 256, 256), :].rearrange("(f p) n -> p f n", p=P)

        block = ctx.enter_context(nc.Block())

        @block.sync
        def _(sp):
            def load(s, src, k, n):
                free = before(SLOT_UNITS, k, s) + n
                if not isinstance(free, int) or free > 0:
                    sp.wait_ge(w_lo_done[s], free)
                sp.dma_start(raw[s][:].rearrange("p (a n) -> p a n", a=src.shape[1]), src).then_inc(raw_full[s], 16)

            def first_units(k, slots=(0, 1)):
                kind, layer, idx = stages[k]
                units = {"ffn": lambda: (col_units(w_gate[layer, idx // 2], 0), col_units(w_up[layer, idx // 2], 0)),
                         "conv": lambda: (col_units(conv_in[0], D), col_units(conv_in[0], 2 * D)),
                         "attn": lambda: (col_units(mix_in[0], 3 * SB_W), col_units(mix_in[0], 3 * SB_W + 256))}[kind]()
                for s in slots:
                    load(s, units[s], k, 0)

            def sb_col(p, n):
                at = p * P + n * SB_W
                return at if isinstance(at, int) else sp.snap(at)

            def sb_units(k, p):
                view = mix_in[0].rearrange("(k p) n -> p k n", p=P)
                sp.wait_ge(w_lo_done[0], p + (before(SLOT_UNITS, k, 0) + 2))
                for n in range(2):
                    sp.dma_start(raw[0][:].rearrange("p (k n) -> p k n", k=KT)[:, :, n * P:(n + 1) * P],
                                 view[:, :, bass.ds(sb_col(p, n), P)]).then_inc(raw_full[0], 16)
                at = sb_col(p, 2)
                sp.wait_ge(w_lo_done[1], p + (before(SLOT_UNITS, k, 1) + 2))
                sp.dma_start(raw[1][:, 0:KT * P].rearrange("p (k n) -> p k n", k=KT),
                             view[:, :, bass.ds(at, P)]).then_inc(raw_full[1], 16)

            def mla_units(k, p):
                sp.wait_ge(w_lo_done[0], p + (before(SLOT_UNITS, k, 0) + 6))
                sp.dma_start(raw[0][:, 0:6 * 192].rearrange("p (k n) -> p k n", k=6),
                             w_uq[0].rearrange("(k p) n -> p k n", p=P)[:, :, bass.ds(p * 192, 192)]).then_inc(raw_full[0], 16)
                at = sp.snap(p * 256) if not isinstance(p, int) else p * 256
                sp.wait_ge(w_lo_done[1], p + (before(SLOT_UNITS, k, 1) + 6))
                sp.dma_start(raw[1][:, 0:2 * 256].rearrange("p (k n) -> p k n", k=2),
                             w_ukv[0].rearrange("(k p) n -> p k n", p=P)[:, :, bass.ds(at, 256)]).then_inc(raw_full[1], 16)

            def load_x(t):
                sp.dma_start(xn[:, t, :], x[0, t * P:(t + 1) * P, :]).then_inc(x_in[t], 16)

            sp.dma_start(ident, consts[:, C_IDENT:C_IDENT + P]).then_inc(ident_in, 16)
            load_x(0)
            first_units(0, (0,))
            load_x(1)
            first_units(0, (1,))
            load_x(2)
            load_x(3)
            sp.dma_start(cst[:, P:], consts[:, P:]).then_inc(consts_in, 16)
            sp.dma_start(rope_sb[HD:P, :], rope).then_inc(consts_in, 16)
            sp.dma_start(rows[ROWS_TAPS:ROWS_QG, :], conv_w[0].rearrange("k (c p) -> (k c) p", p=P)).then_inc(consts_in, 16)
            sp.dma_start(rows[ROWS_QG:ROWS_KVG, :], q_norm_g[0].rearrange("(c p) -> c p", p=P)).then_inc(consts_in, 16)
            sp.dma_start(rows[ROWS_KVG:N_ROWS, :], kv_norm_g[0].rearrange("(c p) -> c p", p=P)).then_inc(consts_in, 16)
            for k, (kind, layer, idx) in enumerate(stages):
                if kind == "ffn":
                    j = idx // 2
                    load(2, row_units(w_down[layer, j], DOWN_UNITS - 1), k, 0)
                    with sp.Fori(1, PAIRS) as i:
                        load(0, col_units(w_gate[layer, j], i * 256), k, i)
                        load(1, col_units(w_up[layer, j], i * 256), k, i)
                    with sp.Fori(0, (DOWN_UNITS - 1) // 2) as i:
                        load(0, row_units(w_down[layer, j], i * 2), k, i + PAIRS)
                        load(1, row_units(w_down[layer, j], i * 2 + 1), k, i + PAIRS)
                if kind == "conv":
                    load(2, col_units(conv_in[0], 0), k, 0)
                    with sp.Fori(0, KT // 2 - 1) as i:
                        load(0, col_units(conv_in[0], i * 256 + (D + 256)), k, i + 1)
                        load(1, col_units(conv_in[0], i * 256 + (2 * D + 256)), k, i + 1)
                        load(2, col_units(conv_in[0], i * 256 + 256), k, i + 1)
                    for u, (s, n) in enumerate(((0, 4), (1, 4), (2, 4), (0, 5))):
                        load(s, row_units(conv_out[0], u), k, n)
                if kind == "attn":
                    w0, w1, w2 = (before(SLOT_UNITS, k, s) for s in range(3))
                    if w2:
                        sp.wait_ge(w_lo_done[2], w2)
                    sp.dma_start(raw[2][:, 0:KT * ROPE].rearrange("p (k n) -> p k n", k=KT),
                                 mix_in[0].rearrange("(k p) n -> p k n", p=P)[:, :, 3 * SB_W + D:]).then_inc(raw_full[2], 16)
                    load(0, col_units(mix_in[0], 3 * SB_W + 512), k, 1)
                    load(1, col_units(mix_in[0], 3 * SB_W + 768), k, 1)
                    with sp.Fori(0, HEAD_PAIRS) as p:
                        sb_units(k, p)
                    with sp.Fori(0, HEAD_PAIRS) as p:
                        mla_units(k, p)
                    load(0, row_units(mix_out[0], 0), k, 10)
                    load(1, row_units(mix_out[0], 1), k, 10)
                    sp.wait_ge(mla_pv_done, 2 * HEAD_PAIRS)
                    load(2, row_units(mix_out[0], 2), k, 1)
                    load(0, row_units(mix_out[0], 3), k, 11)
                if k + 1 < n_stages:
                    first_units(k + 1)
            for t in range(TT):
                sp.wait_ge(x_done, TT * (n_stages - 1) + t + 1)
                sp.dma_start(out[0, t * P:(t + 1) * P, :], xn[:, t, :]).then_inc(out_stored, 16)
            sp.wait_ge(out_stored, 16 * TT)

        @block.tensor
        def _(pe):
            def product3(dst, left, right, first, last):
                pe.matmul(dst, left[0], right[0], start=first, stop=False)
                pe.matmul(dst, left[0], right[1], start=False, stop=False)
                return pe.matmul(dst, left[1], right[0], start=False, stop=last)

            def project_up(bank, s, c):
                hi, lo = up_view[s]
                for kt in range(KT):
                    mm = product3(ps[:, bank, :], (hi[:, kt, c * P:(c + 1) * P], lo[:, kt, c * P:(c + 1) * P]),
                                  (xT_hi[:, kt, :], xT_lo[:, kt, :]), kt == 0, kt == KT - 1)
                return mm

            def project_tokens(bank, s, c, t0, t1):
                hi, lo = up_view[s]
                cut = slice(t0 * P, t1 * P)
                for kt in range(KT):
                    left = [w[:, kt, c * P:(c + 1) * P] for w in (hi, lo)]
                    for n, (a, b) in enumerate(((0, xT_hi), (0, xT_lo), (1, xT_hi))):
                        mm = pe.matmul(ps[:, bank, cut], left[a], b[:, kt, cut], start=t0 == kt == n == 0,
                                       stop=kt == KT - 1 and n == 2, skip_group_check=True)
                return mm

            def head(k, done0, done1):
                pe.wait_ge(xT_ready, 8 * k + 4)
                pe.wait_ge(w_lo_done[0], before(SLOT_UNITS, k, 0) + 1)
                for c in range(2):
                    project_tokens(c, 0, c, 0, 2)
                turn(k, 3)
                pe.wait_ge(xT_ready, 8 * k + 6)
                pe.wait_ge(w_lo_done[1], before(SLOT_UNITS, k, 1) + 1)
                for c in range(2):
                    project_tokens(2 + c, 1, c, 0, 3)
                pe.wait_ge(xT_ready, 8 * k + 8)
                for c in range(2):
                    project_tokens(c, 0, c, 2, 4).then_inc(done0, 1)
                for c in range(2):
                    project_tokens(2 + c, 1, c, 3, 4).then_inc(done1, 1)

            def project_down(t, half, s, f, first, last):
                hi, lo = down_view[s]
                return product3(ps[:, 2 * t + half, :],
                                (left_hi[s][:, f, t * P:(t + 1) * P], left_lo[s][:, f, t * P:(t + 1) * P]),
                                (hi[:, f, half * HALF:(half + 1) * HALF], lo[:, f, half * HALF:(half + 1) * HALF]),
                                first, last)

            def wait_down_unit(k, s, w_n, left_n):
                pe.wait_ge(w_lo_done[s], w_n + (before(SLOT_UNITS, k, s) + 1))
                pe.wait_ge(left_lo_done[s], left_n + (before(LEFT_UNITS, k, s) + 1))

            def down_unit(k, s, order, first=False):
                if first and stages[k][0] == "attn":
                    banks_evacuated(k)
                for t in order:
                    if first and stages[k][0] == "conv" and t < 3:
                        read, n = ((c_copied, KT), (u_done, KT), (conv_out_done, KT))[t]
                        pe.wait_ge(read, n + 2)
                    if first and t == 0 and stages[k][0] == "ffn":
                        banks_evacuated(k)
                    for half in range(2):
                        for f in range(2):
                            mm = project_down(t, half, s, f, first and f == 0, False)
                mm.then_inc(down_used, 1)

            def banks_evacuated(k):
                kind = stages[k][0]
                if kind == "ffn":
                    pe.wait_ge(h_done, FT * (ffns_before(k) + 1) + 2)
                    if k == 0:
                        pe.wait_ge(cols_ready, 1)
                if kind == "attn":
                    pe.wait_ge(mla_oA_copied, HEAD_PAIRS)
                    pe.wait_ge(mla_oB_copied, HEAD_PAIRS)

            def sb_query(k, n):
                pe.wait_ge(w_lo_done[0], n + (before(SLOT_UNITS, k, 0) + 3))
                project_up(6, 0, 0).then_inc(sbq_done, 1)

            def sb_key(n):
                pe.wait_ge(sbq_ready, n + 1)
                project_up(6, 0, 1).then_inc(sbk_done, 1)

            def sb_value(k, n):
                pe.wait_ge(w_lo_done[1], n + (before(SLOT_UNITS, k, 1) + 3))
                pe.wait_ge(sbk_ready, n + 1)
                hi, lo = (w[1][:, 0:KT * P].rearrange("p (k n) -> p k n", k=KT) for w in (w_hi, w_lo))
                for kt in range(KT):
                    mm = product3(ps[:, 6, :], (hi[:, kt, :], lo[:, kt, :]), (xT_hi[:, kt, :], xT_lo[:, kt, :]),
                                  kt == 0, kt == KT - 1)
                mm.then_inc(sbv_done, 1)

            def sb_value_turn(n):
                pe.wait_ge(sb_vT_copied, n + 1)
                for t in range(TT):
                    mm = pe.transpose(ps[:, 5, t * P:(t + 1) * P], sb_vT[:, t * P:(t + 1) * P], ident)
                mm.then_inc(sb_v_turned, 1)

            def sb_pair(k, p, more):
                for a in range(2):
                    rows_a = slice(HD * a, HD * a + HD)
                    if a == 0:
                        pe.wait_ge(sbk_ready, p + 1)
                        pe.wait_ge(sbq_ready, p + 1)
                    else:
                        pe.wait_ge(sb_v_ready, p + 1)
                    for i in range(TT):
                        at, w = Z_AT[i], S - P * i
                        left = [t[rows_a, i * P:(i + 1) * P] for t in sbk]
                        right = [t[rows_a, i * P:S] for t in sbq]
                        dst = z[a][:, at:at + w]
                        pe.matmul(dst, left[0], right[0], start=i < 3, stop=False, skip_group_check=True)
                        pe.matmul(dst, left[0], right[1], start=False, stop=False, skip_group_check=True)
                        mm = pe.matmul(dst, left[1], right[0], start=False, stop=False, skip_group_check=True)
                    mm.then_inc(z_done, 1)
                if more:
                    pe.wait_ge(sb_vT_copied, p + 1)
                    sb_query(k, p + 1)
                for a in range(2):
                    pe.wait_ge(keep_ready, p * 2 + (a + 1))
                    for i in range(TT):
                        at, w = Z_AT[i], S - P * i
                        pe.matmul(z[a][:, at:at + P], ident_r[:], not_past_r[:], start=False, stop=False,
                                  skip_group_check=True)
                        for j in range(i, TT):
                            tri = C_NEG_TRI if j == i else C_NEG_ONES
                            wj = S - P * j
                            mm = pe.matmul(z[a][:, at + P * (j - i):at + w], cst[:, tri:tri + P],
                                           stick[a][:, Z_AT[j]:Z_AT[j] + wj], start=False,
                                           stop=j == TT - 1, skip_group_check=True)
                    mm.then_inc(stick_done, 1)
                    if more and a == 0:
                        sb_key(p + 1)
                for a in range(2):
                    pe.wait_ge(sb_w_done, p * 2 + (a + 1))
                    if a == 1:
                        pe.wait_ge(sb_oA_copied, p + 1)
                    for i in range(TT):
                        mm = pe.matmul(ps[:, 7, i * P:S], sb_v[:, i, :], stick[a][:, Z_AT[i]:Z_AT[i] + S - P * i],
                                       start=i == 0, stop=i == TT - 1)
                    mm.then_inc(sb_pv_done, 1)
                    if more and a == 0:
                        sb_value(k, p + 1)
                if more:
                    sb_value_turn(p + 1)
                pe.wait_ge(sb_oB_copied, p + 1)

            def mla_query(k, n, a):
                pe.wait_ge(w_lo_done[0], n + (before(SLOT_UNITS, k, 0) + 7))
                hi, lo = (w[0][:, 0:6 * 256].rearrange("p (k n) -> p k n", k=6) for w in (w_hi, w_lo))
                for kt in range(6):
                    mm = product3(ps[:, 6 + a, :], (hi[:, kt, a * P:(a + 1) * P], lo[:, kt, a * P:(a + 1) * P]),
                                  (xT_hi[:, kt, :], xT_lo[:, kt, :]), kt == 0, kt == 5)
                mm.then_inc(mq_done, 1)

            def mla_kv(k, n, part, done):
                pe.wait_ge(w_lo_done[1], n + (before(SLOT_UNITS, k, 1) + 7))
                hi, lo = (w[1][:, 0:2 * 256].rearrange("p (k c n) -> p k c n", k=2, c=2) for w in (w_hi, w_lo))
                for kt in range(2):
                    mm = product3(ps[:, 6, :], (hi[:, kt, part, :], lo[:, kt, part, :]),
                                  (xT_hi[:, 6 + kt, :], xT_lo[:, 6 + kt, :]), kt == 0, kt == 1)
                mm.then_inc(done, 1)

            def mla_key(k, n):
                pe.wait_ge(mq_rope_ready, n * 2 + 1)
                pe.wait_ge(mq_nope_copied, n * 2 + 1)
                mla_kv(k, n, 0, mk_done)

            def mla_value(k, n):
                pe.wait_ge(mk_copied, n * 2 + 2)
                mla_kv(k, n, 1, mv_done)

            def mla_value_turn(n):
                pe.wait_ge(mvT_copied, n + 1)
                for t in range(TT):
                    mm = pe.transpose(ps[:, 3, t * P:(t + 1) * P], mla_vT[:, t * P:(t + 1) * P], ident)
                mm.then_inc(mv_turned, 1)

            def mla_scores(p, a, t):
                if a == 1:
                    pe.wait_ge(exp_done, p * 8 + (t + 1))
                if t == 0:
                    pe.wait_ge(mq_rope_ready, p * 2 + (a + 1))
                    pe.wait_ge(mq_nope_copied, p * 2 + (a + 1))
                    pe.wait_ge(mk_copied, p * 2 + (a + 1))
                if a == 0 and t == 3:
                    pe.wait_ge(mv_ready, p + 1)
                keys = P * (t + 1)
                pe.matmul(ps[:, t, 0:keys], mq[a][0:MLA_HEAD_Q, t * P:(t + 1) * P], mk[a][0:MLA_HEAD_Q, 0:keys],
                          start=True, stop=True).then_inc(s_done, 1)

            def mla_turn(p, a, t):
                n = 4 * a + t
                pe.wait_ge(p_ready, p * 8 + (n + 1))
                if n >= 2:
                    pe.wait_ge(pT_copied, p * 8 + (n - 1))
                for kt in range(t + 1):
                    mm = pe.transpose(ps[:, 4 + n % 2, kt * P:(kt + 1) * P], prob[t][:, kt * P:(kt + 1) * P], ident)
                mm.then_inc(p_turned, 1)

            def mla_mix(p, a):
                pe.wait_ge(pT_copied, p * 8 + 4 * (a + 1))
                for kt in range(TT):
                    mm = pe.matmul(ps[:, 7, kt * P:S], mv[:, kt, :], pT[a][:, kt, kt * P:S],
                                   start=kt == 0, stop=kt == TT - 1)
                mm.then_inc(mla_pv_done, 1)

            def mla_pair(k, p, more):
                for t in range(TT):
                    mla_scores(p, 0, t)
                if more:
                    mla_query(k, p + 1, 0)
                mla_turn(p, 0, 0)
                mla_turn(p, 0, 1)
                mla_scores(p, 1, 0)
                mla_scores(p, 1, 1)
                mla_turn(p, 0, 2)
                mla_turn(p, 0, 3)
                mla_scores(p, 1, 2)
                mla_scores(p, 1, 3)
                if more:
                    mla_query(k, p + 1, 1)
                mla_turn(p, 1, 0)
                mla_turn(p, 1, 1)
                if more:
                    mla_key(k, p + 1)
                mla_turn(p, 1, 2)
                mla_turn(p, 1, 3)
                if more:
                    pe.wait_ge(mq_rope_ready, p * 2 + 4)
                    pe.wait_ge(mq_nope_copied, p * 2 + 4)
                mla_mix(p, 0)
                if more:
                    mla_value(k, p + 1)
                pe.wait_ge(mla_oA_copied, p + 1)
                mla_mix(p, 1)
                if more:
                    mla_value_turn(p + 1)
                    pe.wait_ge(mla_oB_copied, p + 1)

            def latents(k):
                head(k, lat_done, lat_done)
                pe.wait_ge(w_lo_done[2], before(SLOT_UNITS, k, 2) + 1)
                hi, lo = (w[2][:, 0:KT * P].rearrange("p (k n) -> p k n", k=KT) for w in (w_hi, w_lo))
                for kt in range(KT):
                    mm = product3(ps[:, 4, :], (hi[:, kt, :], lo[:, kt, :]), (xT_hi[:, kt, :], xT_lo[:, kt, :]),
                                  kt == 0, kt == KT - 1)
                mm.then_inc(kr_done, 1)
                for u in range(2, LATENT_UNITS):
                    pe.wait_ge(w_lo_done[u % 2], before(SLOT_UNITS, k, u % 2) + u // 2 + 1)
                    for c in range(2):
                        ct = 2 * u + c
                        if ct == 7:
                            pe.wait_ge(lat_squared, 1)
                        project_up(LAT_BANK[ct], u % 2, c).then_inc(lat_done, 1)
            def latent_sums():
                for n, tiles in enumerate((6, 8)):
                    pe.wait_ge(sq_added, tiles)
                    pe.matmul(ps[:, 1 + n, :], cst[:, C_NEG_ONES:C_NEG_ONES + P], sq_sum[n],
                              start=True, stop=True).then_inc(sum_done, 1)

            def turn(m, t):
                if m == 0:
                    pe.wait_ge(x_in[t], 16)
                else:
                    pe.wait_ge(x_done, TT * (m - 1) + t + 1)
                for kt in range(KT):
                    mm = pe.transpose(ps[:, 2 * t + kt // 4, (kt % 4) * P:(kt % 4 + 1) * P],
                                      xn[:, t, kt * P:(kt + 1) * P], ident)
                    if kt % 4 == 3:
                        mm.then_inc(turned, 1)

            def tail(k, order, w_n, left_n):
                more = k + 1 < n_stages

                def part(t, s, halves=(0, 1)):
                    for half in halves:
                        for f in range(2):
                            mm = project_down(t, half, s, f, False, s == last and f == 1)
                        if s == last:
                            mm.then_inc(y_done, 1)
                    return mm

                last = order[2]
                for t, s in ((0, order[0]), (0, order[1]), (1, order[0]), (0, last), (1, order[1]), (1, last)):
                    if t == 0:
                        wait_down_unit(k, s, w_n[s], left_n[s])
                    part(t, s)
                for half in range(2):
                    for s in order:
                        part(2, s, (half,))
                    if more:
                        turn(k + 1, half)
                last = 2
                for s in range(3):
                    mm = part(3, s)
                    if s < 2:
                        mm.then_inc(down_used, 1)
                if more:
                    turn(k + 1, 2)

            pe.wait_ge(ident_in, 16)
            for t in range(3):
                turn(0, t)

            for k, (kind, layer, idx) in enumerate(stages):
                w0, w1, w2 = (before(SLOT_UNITS, k, s) for s in range(3))
                if kind == "ffn":
                    p0 = FT * ffns_before(k)
                    head(k, gate_done, up_done)
                    if k == 0:
                        pe.wait_ge(consts_in, 80)
                        pe.transpose(ps[:, 7, 0:N_ROWS], rows[:],
                                     cst[0:N_ROWS, C_IDENT:C_IDENT + N_ROWS]).then_inc(rows_turned, 1)
                    with pe.Fori(1, PAIRS) as i:
                        pe.wait_ge(w_lo_done[0], i + (w0 + 1))
                        for c in range(2):
                            pe.wait_ge(silu_done, i * 2 + (p0 + 1 + c))
                            project_up(c, 0, c).then_inc(gate_done, 1)
                        pe.wait_ge(w_lo_done[1], i + (w1 + 1))
                        for c in range(2):
                            pe.wait_ge(h_done, i * 2 + (p0 + 1 + c))
                            project_up(2 + c, 1, c).then_inc(up_done, 1)
                    for u in range(2):
                        wait_down_unit(k, u, PAIRS, 0)
                        down_unit(k, u, (2, 3, 0, 1), first=u == 0)
                    with pe.Fori(1, (DOWN_UNITS - 3) // 2) as i:
                        for s in range(2):
                            wait_down_unit(k, s, i + PAIRS, i)
                            down_unit(k, s, range(TT))
                    tail(k, FFN_TAIL, (15, 15, 0), (4, 4, 0))
                if kind == "conv":
                    head(k, conv_c_done, conv_h_done)
                    pe.wait_ge(w_lo_done[2], w2 + 1)
                    for c in range(2):
                        project_up(4 + c, 2, c).then_inc(conv_b_done, 1)
                    with pe.Fori(1, KT // 2) as i:
                        for s, (read, done) in enumerate(((c_copied, conv_c_done), (u_done, conv_h_done),
                                                          (conv_out_done, conv_b_done))):
                            pe.wait_ge(w_lo_done[s], i + (before(SLOT_UNITS, k, s) + 1))
                            for c in range(2):
                                pe.wait_ge(read, i * 2 + (1 + c))
                                project_up(2 * s + c, s, c).then_inc(done, 1)
                    wait_down_unit(k, 0, 4, 0)
                    down_unit(k, 0, (3, 0, 1, 2), first=True)
                    tail(k, MIX_TAIL, (5, 4, 4), (1, 0, 0))
                if kind == "attn":
                    latents(k)
                    pe.wait_ge(lat_squared, 7)
                    sb_query(k, 0)
                    sb_key(0)
                    latent_sums()
                    sb_value(k, 0)
                    sb_value_turn(0)
                    pe.wait_ge(lat_squared, KT)
                    pe.wait_ge(kr_step, 3)
                    pe.wait_ge(rms_ready, 2)
                    with pe.Fori(0, HEAD_PAIRS - 1) as p:
                        sb_pair(k, p, True)
                    sb_pair(k, HEAD_PAIRS - 1, False)
                    pe.wait_ge(lat_ready, KT)
                    mla_query(k, 0, 0)
                    mla_query(k, 0, 1)
                    mla_key(k, 0)
                    mla_value(k, 0)
                    pe.wait_ge(mq_rope_ready, 2)
                    mla_value_turn(0)
                    with pe.Fori(0, HEAD_PAIRS - 1) as p:
                        mla_pair(k, p, True)
                    mla_pair(k, HEAD_PAIRS - 1, False)
                    wait_down_unit(k, 0, 10, 0)
                    down_unit(k, 0, (3, 0, 1, 2), first=True)
                    tail(k, MIX_TAIL, (11, 10, 1), (1, 0, 0))

        @block.scalar
        def _(act):
            def split_w(k, s, n, width=UNIT, dmas=None):
                arrived = n + (before(SLOT_DMAS, k, s) + 1) if dmas is None else dmas
                act.wait_ge(raw_full[s], arrived * 16)
                act.activation(w_hi[s][:, 0:width], raw[s][:, 0:width], ACT.Copy).then_inc(w_hi_done[s], 1)

            def split_left(s, f):
                act.activation(left_hi[s][:], h[:, bass.ds(f, 2), :], ACT.Copy).then_inc(left_hi_done[s], 1)

            def turn_hi(m, t):
                for half in range(2):
                    act.wait_ge(turned, 8 * m + 2 * t + half + 1)
                    act.activation(xT_hi[:, 4 * half:4 * half + 4, t * P:(t + 1) * P],
                                   ps[:, 2 * t + half, :].rearrange("p (k n) -> p k n", k=4),
                                   ACT.Copy).then_inc(xT_hi_done, 1)

            def close_stage(k):
                if k + 1 == n_stages:
                    return
                turn_hi(k + 1, 0)
                turn_hi(k + 1, 1)
                act.wait_ge(down_used, before(DOWN_USED, k + 1) - 1)
                split_w(k + 1, 0, 0)
                act.wait_ge(down_used, before(DOWN_USED, k + 1))
                split_w(k + 1, 1, 0)
                turn_hi(k + 1, 2)
                turn_hi(k + 1, 3)

            def rotary_views(dst, src, kts, heads, lead):
                half = ROPE // 2
                d = dst.rearrange("p (k a n) -> p k a n", k=kts, a=heads)
                r = src.rearrange("p (k a n) -> p k a n", k=kts, a=heads)
                return ((d[:, :, :, HD - lead:HD + ROPE], r),
                        (d[:, :, :, HD + ROPE:HD + ROPE + half], r[:, :, :, lead + half:lead + ROPE]),
                        (d[:, :, :, HD + ROPE + half:P], r[:, :, :, lead:lead + half]))

            def split_rotary(k, s, n, kts, heads, lead):
                act.wait_ge(raw_full[s], (n + (before(SLOT_DMAS, k, s) + 1)) * 16)
                for dst, src in rotary_views(w_hi[s][:, 0:kts * heads * P],
                                             raw[s][:, 0:kts * heads * (lead + ROPE)], kts, heads, lead):
                    last = act.activation(dst, src, ACT.Copy)
                last.then_inc(w_hi_done[s], 1)

            def split_kv(k, n):
                act.wait_ge(raw_full[1], (n + (before(SLOT_DMAS, k, 1) + 1)) * 16)
                for part in range(2):
                    last = act.activation(kv_view(w_hi[1], part), kv_raw(part), ACT.Copy)
                last.then_inc(w_hi_done[1], 1)

            def latent_tiles(k):
                for ct in range(KT):
                    act.wait_ge(lat_done, ct + 1)
                    act.activation(latent[ct], ps[:, LAT_BANK[ct], :], ACT.Copy)
                    if ct >= 2:
                        act.wait_ge(sq_added, ct - 1)
                    act.activation(gs[:, ct % 2, :], ps[:, LAT_BANK[ct], :], ACT.Square).then_inc(lat_squared, 1)
                    if ct == 1:
                        split_w(k, 0, 1)
                        split_rotary(k, 2, 0, KT, 1, 0)
                    if ct == 3:
                        split_w(k, 1, 1)
                    if ct == 5:
                        split_w(k, 0, 2, dmas=before(SLOT_DMAS, k, 0) + 4)
                split_w(k, 1, 2, width=KT * P)

            def sb_query_hi(n):
                act.wait_ge(sbq_done, n + 1)
                act.activation(sbq[0], ps[:, 6, :], ACT.Copy, scale=HD ** -0.5).then_inc(sbq_hi_done, 1)

            def sb_key_hi(n):
                act.wait_ge(sbk_done, n + 1)
                act.activation(sbk[0], ps[:, 6, :], ACT.Copy).then_inc(sbk_hi_done, 1)

            def sb_value_copy(n):
                act.wait_ge(sbv_done, n + 1)
                act.activation(sb_vT, ps[:, 6, :], ACT.Copy).then_inc(sb_vT_copied, 1)

            def sb_pair(k, p, more):
                if more:
                    act.wait_ge(raw_full[0], p * 32 + 16 * (before(SLOT_DMAS, k, 0) + 6))
                    act.activation(w_hi[0][:], raw[0][:], ACT.Copy).then_inc(w_hi_done[0], 1)
                else:
                    split_rotary(k, 0, 10, 6, 2, HD)
                for a in range(2):
                    act.wait_ge(z_done, p * 2 + (a + 1))
                    act.activation(stick[a], z[a], ACT.Abs).then_inc(soft_step, 1)
                    act.wait_ge(soft_step, p * 4 + (2 * a + 1))
                    act.activation(stick[a], stick[a], ACT.Exp, scale=-1.0).then_inc(soft_step, 1)
                    act.wait_ge(soft_step, p * 4 + (2 * a + 2))
                    act.activation(stick[a], stick[a], ACT.Ln, bias=1.0).then_inc(log_ready, 1)
                if more:
                    split_w(k, 1, p + 3, width=KT * P)
                    sb_query_hi(p + 1)
                else:
                    split_kv(k, 6)
                act.wait_ge(stick_done, p * 2 + 1)
                act.activation(stick[0], z[0], ACT.Exp).then_inc(sb_w_done, 1)
                if more:
                    sb_key_hi(p + 1)
                act.wait_ge(stick_done, p * 2 + 2)
                act.activation(stick[1], z[1], ACT.Exp).then_inc(sb_w_done, 1)
                act.wait_ge(sb_pv_done, p * 2 + 1)
                act.activation(h[0:HD, bass.ds(p, 1), :], ps[0:HD, 7:8, :], ACT.Copy).then_inc(sb_oA_copied, 1)
                if more:
                    sb_value_copy(p + 1)

            def latent_hi():
                for ct in range(KT):
                    act.wait_ge(lat_scaled, ct + 1)
                    act.activation(xT_hi[:, ct, :], latent[ct], ACT.Copy).then_inc(lat_hi_done, 1)

            def mla_query_copy(n, a):
                act.wait_ge(mq_done, n * 2 + (a + 1))
                act.activation(mq[a][0:HD, :], ps[0:HD, 6 + a, :], ACT.Copy).then_inc(mq_nope_copied, 1)

            def mla_key_copy(n):
                act.wait_ge(mk_done, n + 1)
                for a in range(2):
                    act.activation(mk[a][0:HD, :], ps[HD * a:HD * a + HD, 6, :], ACT.Copy).then_inc(mk_copied, 1)

            def mla_value_copy(n):
                act.wait_ge(mv_done, n + 1)
                act.activation(mla_vT, ps[:, 6, :], ACT.Copy).then_inc(mvT_copied, 1)

            def mla_exp(p, a, t):
                act.wait_ge(max_ready, p * 8 + (4 * a + t + 1))
                if a == 1:
                    act.wait_ge(p_turned, p * 8 + (t + 1))
                keys = P * (t + 1)
                act.activation(prob[t][:, 0:keys], ps[:, t, 0:keys], ACT.Exp, bias=neg_max[:, t:t + 1],
                               accum_out=p_sum[:, t:t + 1]).then_inc(exp_done, 1)

            def mla_turned_copy(p, a, t):
                n = 4 * a + t
                act.wait_ge(p_turned, p * 8 + (n + 1))
                act.activation(pT[a][:, 0:t + 1, t * P:(t + 1) * P],
                               ps[:, 4 + n % 2, 0:P * (t + 1)].rearrange("p (k n) -> p k n", n=P),
                               ACT.Copy).then_inc(pT_copied, 1)

            def mla_pair(k, p, more):
                if more:
                    split_rotary(k, 0, p + 11, 6, 2, HD)
                    split_kv(k, p + 7)
                else:
                    split_w(k, 0, 10, dmas=before(SLOT_DMAS, k, 0) + 15)
                    split_w(k, 1, 10)
                for t in range(TT):
                    mla_exp(p, 0, t)
                if more:
                    mla_query_copy(p + 1, 0)
                mla_turned_copy(p, 0, 0)
                mla_turned_copy(p, 0, 1)
                mla_exp(p, 1, 0)
                mla_exp(p, 1, 1)
                mla_turned_copy(p, 0, 2)
                mla_turned_copy(p, 0, 3)
                mla_exp(p, 1, 2)
                mla_exp(p, 1, 3)
                if more:
                    mla_query_copy(p + 1, 1)
                mla_turned_copy(p, 1, 0)
                mla_turned_copy(p, 1, 1)
                if more:
                    mla_key_copy(p + 1)
                mla_turned_copy(p, 1, 2)
                mla_turned_copy(p, 1, 3)
                act.wait_ge(mla_pv_done, p * 2 + 1)
                act.activation(h[0:HD, bass.ds(p + 4, 1), :], ps[0:HD, 7:8, :], ACT.Copy).then_inc(mla_oA_copied, 1)
                if more:
                    mla_value_copy(p + 1)

            act.sem_inc(silu_done, 2)
            act.sem_inc(c_copied, 2)
            turn_hi(0, 0)
            split_w(0, 0, 0)
            turn_hi(0, 1)
            split_w(0, 1, 0)
            turn_hi(0, 2)
            turn_hi(0, 3)
            act.wait_ge(consts_in, 80)
            act.activation(ident_r[:], ident, ACT.Copy).then_inc(masks_ready, 1)
            act.activation(not_past_r[:], cst[:, C_NOT_PAST:C_NOT_PAST + P], ACT.Copy).then_inc(masks_ready, 1)

            for k, (kind, layer, idx) in enumerate(stages):
                d0 = before(DOWN_USED, k)
                if kind == "ffn":
                    p0 = FT * ffns_before(k)

                    def silu_pair(i):
                        for c in range(2):
                            act.wait_ge(gate_done, i * 2 + (p0 + 1 + c))
                            act.wait_ge(h_done, i * 2 + (p0 + 1 + c))
                            act.activation(gs[:, c, :], ps[:, c, :], ACT.Silu).then_inc(silu_done, 1)

                    def split_next(i):
                        act.wait_ge(gate_done, i * 2 + (p0 + 2))
                        split_w(k, 0, i + 1)
                        act.wait_ge(up_done, i * 2 + (p0 + 2))
                        split_w(k, 1, i + 1)

                    with act.Fori(0, PAIRS - 1) as i:
                        silu_pair(i)
                        split_next(i)
                    if k > 0:
                        act.wait_ge(y_done, 8 * k)
                    act.wait_ge(h_done, p0 + 4 + 2)
                    for s in range(2):
                        split_left(s, 2 * s)
                    silu_pair(PAIRS - 1)
                    split_next(PAIRS - 1)
                    split_w(k, 2, 0)
                    act.wait_ge(h_done, p0 + FT + 2)
                    split_left(2, FT - 2)
                    with act.Fori(1, (DOWN_UNITS - 1) // 2) as i:
                        for s in range(2):
                            act.wait_ge(down_used, i * 2 + (d0 + s - 1))
                            split_left(s, i * 4 + 2 * s)
                            split_w(k, s, i + PAIRS)
                if kind == "conv":
                    split_w(k, 2, 0)

                    def conv_pair(i, last):
                        for c in range(2):
                            act.wait_ge(conv_c_done, i * 2 + (1 + c))
                            act.wait_ge(u_done, i * 2 + (1 + c))
                            act.activation(gs[:, c, :], ps[:, c, :], ACT.Copy).then_inc(c_copied, 1)
                        for s, done in enumerate((conv_c_done, conv_h_done, conv_b_done)):
                            if last:
                                act.wait_ge(conv_out_done, 2 * s + 4)
                                split_left(s, 2 * s)
                            act.wait_ge(done, i * 2 + 2)
                            split_w(k, s, i + 1)

                    with act.Fori(0, KT // 2 - 1) as i:
                        conv_pair(i, False)
                    conv_pair(KT // 2 - 1, True)
                    act.wait_ge(conv_out_done, KT + 2)
                    act.wait_ge(down_used, d0 + 1)
                    split_left(0, 6)
                    split_w(k, 0, 5)
                if kind == "attn":
                    latent_tiles(k)
                    sb_query_hi(0)
                    sb_key_hi(0)
                    for n, width in enumerate((MLA_SCALE ** 2, 1.0)):
                        act.wait_ge(rms_step, 2 * n + 2)
                        act.activation(sq_sum[n], sq_sum[n], ACT.Sqrt, scale=width).then_inc(rms_ready, 1)
                    sb_value_copy(0)
                    with act.Fori(0, HEAD_PAIRS - 1) as p:
                        sb_pair(k, p, True)
                    sb_pair(k, HEAD_PAIRS - 1, False)
                    latent_hi()
                    for a in range(2):
                        mla_query_copy(0, a)
                    mla_key_copy(0)
                    mla_value_copy(0)
                    with act.Fori(0, HEAD_PAIRS - 1) as p:
                        mla_pair(k, p, True)
                    mla_pair(k, HEAD_PAIRS - 1, False)
                    act.wait_ge(mla_oB_copied, HEAD_PAIRS)
                    for s in range(3):
                        split_left(s, 2 * s)
                    split_w(k, 2, 1)
                    act.wait_ge(down_used, d0 + 1)
                    split_left(0, 6)
                    split_w(k, 0, 11, dmas=before(SLOT_DMAS, k, 0) + 16)
                close_stage(k)

        @block.vector
        def _(dve):
            def split_w(k, s, n, width=UNIT):
                dve.wait_ge(w_hi_done[s], n + (before(SLOT_UNITS, k, s) + 1))
                dve.tensor_tensor(w_lo[s][:, 0:width], raw[s][:, 0:width], w_hi[s][:, 0:width],
                                  ALU.subtract).then_inc(w_lo_done[s], 1)

            def split_left(k, s, n, f):
                dve.wait_ge(left_hi_done[s], n + (before(LEFT_UNITS, k, s) + 1))
                dve.tensor_tensor(left_lo[s][:], h[:, bass.ds(f, 2), :], left_hi[s][:],
                                  ALU.subtract).then_inc(left_lo_done[s], 1)

            def turn_lo(m, t):
                for half in range(2):
                    dve.wait_ge(xT_hi_done, 8 * m + 2 * t + half + 1)
                    k4 = slice(4 * half, 4 * half + 4)
                    dve.tensor_tensor(xT_lo[:, k4, t * P:(t + 1) * P],
                                      ps[:, 2 * t + half, :].rearrange("p (k n) -> p k n", k=4),
                                      xT_hi[:, k4, t * P:(t + 1) * P], ALU.subtract).then_inc(xT_ready, 1)

            def layer_norm(k, t, scale):
                b = 6 * (TT * k + t)
                dve.wait_ge(res_ready, TT * k + t + 1)
                for half in range(2):
                    dve.wait_ge(y_done, 8 * k + 2 * t + half + 1)
                    part = xn[:, t, half * HALF:(half + 1) * HALF]
                    dve.scalar_tensor_tensor(part, ps[:, 2 * t + half, :], scale, part,
                                             ALU.mult, ALU.add).then_inc(ln_step, 1)
                for half in range(2):
                    dve.wait_ge(ln_step, b + half + 1)
                    dve.bn_stats(stats[:, half, :], xn[:, t, half * HALF:(half + 1) * HALF]).then_inc(ln_step, 1)
                dve.wait_ge(ln_step, b + 4)
                dve.bn_aggr(mean_var[:], stats[:].rearrange("p a b -> p (a b)")).then_inc(ln_step, 1)
                dve.wait_ge(ln_step, b + 5)
                dve.tensor_scalar(veps[:], mean_var[:, 1:2], LN_EPS, None, ALU.add).then_inc(var_ready, 1)
                if t == 0:
                    dve.wait_ge(gb_full, 32 * (k + 1))
                dve.scalar_tensor_tensor(xn[:, t, :], xn[:, t, :], mean_var[:, 0:1], gb[:, 0, :],
                                         ALU.subtract, ALU.mult).then_inc(ln_step, 1)
                dve.wait_ge(ln_step, b + 6)
                dve.wait_ge(rstd_ready, TT * k + t + 1)
                dve.scalar_tensor_tensor(xn[:, t, :], xn[:, t, :], rstd[:, t:t + 1], gb[:, 1, :],
                                         ALU.mult, ALU.add).then_inc(x_done, 1)

            def rotary_lo(k, s, n, kts, heads, lead):
                half = ROPE // 2
                dve.wait_ge(w_hi_done[s], n + (before(SLOT_UNITS, k, s) + 1))
                hi, lo = (w[:, 0:kts * heads * P].rearrange("p (k a n) -> p k a n", k=kts, a=heads)
                          for w in (w_hi[s], w_lo[s]))
                r = raw[s][:, 0:kts * heads * (lead + ROPE)].rearrange("p (k a n) -> p k a n", k=kts, a=heads)
                for dst, src in ((slice(HD - lead, HD + ROPE), slice(0, lead + ROPE)),
                                 (slice(HD + ROPE, HD + ROPE + half), slice(lead + half, lead + ROPE)),
                                 (slice(HD + ROPE + half, P), slice(lead, lead + half))):
                    last = dve.tensor_tensor(lo[:, :, :, dst], r[:, :, :, src], hi[:, :, :, dst], ALU.subtract)
                last.then_inc(w_lo_done[s], 1)

            def kv_lo(k, n):
                dve.wait_ge(w_hi_done[1], n + (before(SLOT_UNITS, k, 1) + 1))
                for part in range(2):
                    last = dve.tensor_tensor(kv_view(w_lo[1], part), kv_raw(part), kv_view(w_hi[1], part), ALU.subtract)
                last.then_inc(w_lo_done[1], 1)

            def rotate(dst, bank, base, step, done):
                dve.tensor_tensor(dst[HD:HD + ROPE, :], ps[HD:HD + ROPE, bank, :], rope_sb[HD:HD + ROPE, :],
                                  ALU.mult).then_inc(step, 1)
                dve.tensor_tensor(rope_tmp[HD:HD + ROPE, :], ps[HD + ROPE:P, bank, :], rope_sb[HD + ROPE:P, :],
                                  ALU.mult).then_inc(step, 1)
                dve.wait_ge(step, base + 2)
                dve.tensor_tensor(dst[HD:HD + ROPE, :], dst[HD:HD + ROPE, :], rope_tmp[HD:HD + ROPE, :],
                                  ALU.add).then_inc(done, 1)

            def sb_query_lo(n):
                dve.wait_ge(sbq_hi_done, n + 1)
                dve.scalar_tensor_tensor(sbq[1], ps[:, 6, :], HD ** -0.5, sbq[0],
                                         ALU.mult, ALU.subtract).then_inc(sbq_ready, 1)

            def sb_key_lo(n):
                dve.wait_ge(sbk_hi_done, n + 1)
                dve.tensor_tensor(sbk[1], ps[:, 6, :], sbk[0], ALU.subtract).then_inc(sbk_ready, 1)

            def sb_value_copy(n):
                dve.wait_ge(sb_v_turned, n + 1)
                dve.tensor_copy(sb_v, ps[:, 5, :].rearrange("p (k n) -> p k n", n=P)).then_inc(sb_v_ready, 1)

            def latent_norms():
                for n, width in enumerate((Q_RANK, KV_RANK)):
                    dve.wait_ge(sum_done, n + 1)
                    dve.tensor_scalar(sq_sum[n], ps[:, 1 + n, :], -1.0 / width, RMS_EPS,
                                      ALU.mult, ALU.add).then_inc(rms_step, 1)
                    dve.wait_ge(rms_step, 2 * n + 1)
                    dve.reciprocal(sq_sum[n], sq_sum[n]).then_inc(rms_step, 1)

            def sb_pair(k, p, more):
                if more:
                    split_w(k, 0, p + 3)
                else:
                    rotary_lo(k, 0, 6, 6, 2, HD)
                for a in range(2):
                    dve.wait_ge(log_ready, p * 2 + (a + 1))
                    dve.scalar_tensor_tensor(stick[a], z[a], 0.0, stick[a], ALU.max, ALU.add).then_inc(keep_step, 1)
                    dve.wait_ge(keep_step, p * 4 + (2 * a + 1))
                    past = cst[:, C_PAST:C_PAST + P]
                    last_tile = stick[a][:, Z_AT[3]:Z_AT[3] + P]
                    dve.tensor_tensor(last_tile, last_tile, past, ALU.mult).then_inc(keep_step, 1)
                    for i in range(3):
                        diag = stick[a][:, Z_AT[i]:Z_AT[i] + P]
                        mm = dve.tensor_tensor(diag, diag, past, ALU.mult)
                    mm.then_inc(keep_ready, 1)
                if more:
                    split_w(k, 1, p + 3, width=KT * P)
                    sb_query_lo(p + 1)
                    sb_key_lo(p + 1)
                else:
                    kv_lo(k, 6)
                dve.wait_ge(sb_pv_done, p * 2 + 2)
                dve.tensor_copy(h[HD:P, bass.ds(p, 1), :], ps[HD:P, 7:8, :]).then_inc(sb_oB_copied, 1)
                if more:
                    sb_value_copy(p + 1)

            def latent_scale():
                for ct in range(KT):
                    n = 0 if ct < 6 else 1
                    dve.wait_ge(rms_ready, n + 1)
                    g = cols[:, ROWS_QG + ct:ROWS_QG + ct + 1]
                    dve.scalar_tensor_tensor(latent[ct], latent[ct], g, sq_sum[n], ALU.mult, ALU.mult).then_inc(lat_scaled, 1)

            def latent_lo():
                for ct in range(KT):
                    dve.wait_ge(lat_hi_done, ct + 1)
                    dve.tensor_tensor(xT_lo[:, ct, :], latent[ct], xT_hi[:, ct, :], ALU.subtract).then_inc(lat_ready, 1)

            def mla_query_rope(n, a):
                dve.wait_ge(mq_done, n * 2 + (a + 1))
                dve.wait_ge(mq_nope_copied, n * 2 + (a + 1))
                dve.wait_ge(*((kr_step, 3) if isinstance(n, int) and n + a == 0 else (mq_rope_ready, n * 2 + a)))
                rotate(mq[a], 6 + a, n * 4 + 2 * a, mq_step, mq_rope_ready)

            def mla_max(p, a, t):
                n = 4 * a + t
                dve.wait_ge(s_done, p * 8 + (n + 1))
                diag = ps[:, t, t * P:(t + 1) * P]
                dve.tensor_tensor(diag, diag, cst[:, C_CAUSAL:C_CAUSAL + P], ALU.add).then_inc(max_step, 1)
                dve.wait_ge(max_step, p * 8 + (n + 1))
                dve.tensor_reduce(neg_max[:, t:t + 1], ps[:, t, 0:P * (t + 1)], AX.X, ALU.max,
                                  negate=True).then_inc(max_ready, 1)

            def mla_norm(p, a, t):
                n = 4 * a + t
                dve.wait_ge(exp_done, p * 8 + (n + 1))
                dve.reciprocal(p_sum[:, t:t + 1], p_sum[:, t:t + 1]).then_inc(norm_step, 1)
                dve.wait_ge(norm_step, p * 8 + (n + 1))
                rows_t = prob[t][:, 0:P * (t + 1)]
                dve.tensor_scalar(rows_t, rows_t, p_sum[:, t:t + 1], None, ALU.mult).then_inc(p_ready, 1)

            def mla_value_copy(n):
                dve.wait_ge(mv_turned, n + 1)
                dve.tensor_copy(mv, ps[:, 3, :].rearrange("p (k n) -> p k n", n=P)).then_inc(mv_ready, 1)

            def mla_pair(k, p, more):
                if more:
                    rotary_lo(k, 0, p + 7, 6, 2, HD)
                    kv_lo(k, p + 7)
                else:
                    split_w(k, 0, 10)
                    split_w(k, 1, 10)
                mla_max(p, 0, 0)
                mla_max(p, 0, 1)
                mla_norm(p, 0, 0)
                mla_max(p, 0, 2)
                mla_norm(p, 0, 1)
                mla_max(p, 0, 3)
                mla_norm(p, 0, 2)
                mla_norm(p, 0, 3)
                if more:
                    mla_query_rope(p + 1, 0)
                mla_max(p, 1, 0)
                mla_max(p, 1, 1)
                mla_norm(p, 1, 0)
                mla_norm(p, 1, 1)
                mla_max(p, 1, 2)
                mla_max(p, 1, 3)
                mla_norm(p, 1, 2)
                mla_norm(p, 1, 3)
                if more:
                    mla_query_rope(p + 1, 1)
                dve.wait_ge(mla_pv_done, p * 2 + 2)
                dve.tensor_copy(h[HD:P, bass.ds(p + 4, 1), :], ps[HD:P, 7:8, :]).then_inc(mla_oB_copied, 1)
                if more:
                    mla_value_copy(p + 1)

            def close_stage(k, scale):
                more = k + 1 < n_stages
                layer_norm(k, 0, scale)
                layer_norm(k, 1, scale)
                if more:
                    turn_lo(k + 1, 0)
                layer_norm(k, 2, scale)
                if more:
                    turn_lo(k + 1, 1)
                layer_norm(k, 3, scale)
                if more:
                    turn_lo(k + 1, 2)
                    turn_lo(k + 1, 3)

            dve.sem_inc(h_done, 2)
            dve.sem_inc(u_done, 2)
            dve.sem_inc(conv_out_done, 2)
            turn_lo(0, 0)
            split_w(0, 0, 0)
            turn_lo(0, 1)
            split_w(0, 1, 0)
            turn_lo(0, 2)
            turn_lo(0, 3)
            dve.wait_ge(rows_turned, 1)
            dve.tensor_copy(cols[:], ps[:, 7, 0:N_ROWS]).then_inc(cols_ready, 1)

            for k, (kind, layer, idx) in enumerate(stages):
                if kind == "ffn":
                    p0 = FT * ffns_before(k)

                    def gated_pair(i):
                        for c in range(2):
                            dve.wait_ge(silu_done, i * 2 + (p0 + 3 + c))
                            dve.wait_ge(up_done, i * 2 + (p0 + 1 + c))
                            dve.tensor_tensor(h[:, bass.ds(i * 2 + c, 1), :], gs[:, c:c + 1, :], ps[:, 2 + c:3 + c, :],
                                              ALU.mult).then_inc(h_done, 1)

                    with dve.Fori(0, PAIRS - 1) as i:
                        split_w(k, 0, i + 1)
                        gated_pair(i)
                        split_w(k, 1, i + 1)
                    for s in range(2):
                        split_left(k, s, 0, 2 * s)
                    split_w(k, 0, PAIRS)
                    gated_pair(PAIRS - 1)
                    split_w(k, 1, PAIRS)
                    split_w(k, 2, 0)
                    split_left(k, 2, 0, FT - 2)
                    with dve.Fori(1, (DOWN_UNITS - 1) // 2) as i:
                        for s in range(2):
                            split_left(k, s, i, i * 4 + 2 * s)
                            split_w(k, s, i + PAIRS)
                    close_stage(k, 0.5)
                if kind == "conv":
                    for c in range(2):
                        dve.memset(conv_u[c][:, 0:U_PAD], 0.0).then_inc(u_zeroed, 1)
                    dve.wait_ge(u_zeroed, 2)
                    split_w(k, 2, 0)

                    def conv_tile(i, c):
                        dve.wait_ge(u_done, i * 2 + (3 + c))
                        dve.tensor_scalar(conv_acc[c], conv_u[c][:, 2:2 + S], taps[:, 2, c:c + 1], None,
                                          ALU.mult).then_inc(conv_step, 1)
                        for n, tap in enumerate((1, 0)):
                            dve.wait_ge(conv_step, i * 6 + (3 * c + n + 1))
                            dve.scalar_tensor_tensor(conv_acc[c], conv_u[c][:, tap:tap + S], taps[:, tap, c:c + 1],
                                                     conv_acc[c], ALU.mult, ALU.add).then_inc(conv_step, 1)

                    def conv_pair(i, last):
                        dve.tensor_copy(taps[:], cols[:, ROWS_TAPS:ROWS_QG].rearrange("p (k c) -> p k c", k=3)
                                        [:, :, bass.ds(i * 2, 2)]).then_inc(taps_set, 1)
                        if last:
                            split_left(k, 0, 0, 0)
                        split_w(k, 0, i + 1)
                        dve.wait_ge(taps_set, i + 1)
                        for c in range(2):
                            dve.wait_ge(c_copied, i * 2 + (3 + c))
                            dve.wait_ge(conv_h_done, i * 2 + (1 + c))
                            dve.tensor_tensor(conv_u[c][:, U_PAD:U_PAD + S], gs[:, c, :], ps[:, 2 + c, :],
                                              ALU.mult).then_inc(u_done, 1)
                            conv_tile(i, c)
                        if last:
                            split_left(k, 1, 0, 2)
                        split_w(k, 1, i + 1)
                        for c in range(2):
                            dve.wait_ge(conv_step, i * 6 + (3 * c + 3))
                            dve.wait_ge(conv_b_done, i * 2 + (1 + c))
                            dve.tensor_tensor(h[:, bass.ds(i * 2 + c, 1), :],
                                              conv_acc[c].rearrange("p (a n) -> p a n", a=1),
                                              ps[:, 4 + c:5 + c, :], ALU.mult).then_inc(conv_out_done, 1)
                        if last:
                            split_left(k, 2, 0, 4)
                        split_w(k, 2, i + 1)

                    with dve.Fori(0, KT // 2 - 1) as i:
                        conv_pair(i, False)
                    conv_pair(KT // 2 - 1, True)
                    split_left(k, 0, 1, 6)
                    split_w(k, 0, 5)
                    close_stage(k, 1.0)
                if kind == "attn":
                    split_w(k, 0, 1)
                    rotary_lo(k, 2, 0, KT, 1, 0)
                    split_w(k, 1, 1)
                    dve.wait_ge(kr_done, 1)
                    rotate(k_rope, 4, 0, kr_step, kr_step)
                    split_w(k, 0, 2)
                    split_w(k, 1, 2, width=KT * P)
                    sb_query_lo(0)
                    sb_key_lo(0)
                    latent_norms()
                    sb_value_copy(0)
                    latent_scale()
                    with dve.Fori(0, HEAD_PAIRS - 1) as p:
                        sb_pair(k, p, True)
                    sb_pair(k, HEAD_PAIRS - 1, False)
                    for a in range(2):
                        dve.tensor_copy(mk[a][HD:HD + ROPE, :], k_rope[HD:HD + ROPE, :]).then_inc(k_rope_placed, 1)
                    latent_lo()
                    for a in range(2):
                        mla_query_rope(0, a)
                    mla_value_copy(0)
                    with dve.Fori(0, HEAD_PAIRS - 1) as p:
                        mla_pair(k, p, True)
                    mla_pair(k, HEAD_PAIRS - 1, False)
                    for s in range(3):
                        split_left(k, s, 0, 2 * s)
                    split_w(k, 2, 1)
                    split_left(k, 0, 1, 6)
                    split_w(k, 0, 11)
                    close_stage(k, 1.0)

        @block.gpsimd
        def _(pool):
            pool.memset(half_neg[:], -0.5).then_inc(exp_ready, 1)
            pool.wait_ge(exp_ready, 1)
            for k, (kind, layer, idx) in enumerate(stages):
                if k > 0:
                    pool.wait_ge(x_done, TT * k)
                pool.dma_start(gb[:, 0, :], ln_g[layer, idx].partition_broadcast(P)).then_inc(gb_full, 16)
                pool.dma_start(gb[:, 1, :], ln_b[layer, idx].partition_broadcast(P)).then_inc(gb_full, 16)
                for t in range(TT):
                    pool.wait_ge(turned, 8 * k + 2 * t + 2)
                    pool.tensor_scalar(xn[:, t, :], xn[:, t, :], ALPHA, None, ALU.mult).then_inc(res_ready, 1)
                if kind == "attn":
                    pool.wait_ge(w_lo_done[2], before(SLOT_UNITS, k, 2))
                    for n in range(2):
                        pool.memset(sq_sum[n], 0.0).then_inc(sums_zeroed, 1)
                    for ct in range(KT):
                        n = 0 if ct < 6 else 1
                        pool.wait_ge(lat_squared, ct + 1)
                        if ct in (0, 6):
                            pool.wait_ge(sums_zeroed, 2)
                        else:
                            pool.wait_ge(sq_added, ct)
                        pool.tensor_tensor(sq_sum[n], sq_sum[n], gs[:, ct % 2, :], ALU.add).then_inc(sq_added, 1)
                for t in range(TT):
                    pool.wait_ge(var_ready, TT * k + t + 1)
                    pool.tensor_tensor(rstd[:, t:t + 1], veps[:], half_neg[:], ALU.pow).then_inc(rstd_ready, 1)
                    if t >= 2 and k + 1 < n_stages:
                        s = t - 2
                        pool.wait_ge(w_hi_done[s], before(SLOT_UNITS, k + 1, s) + 1)
                        pool.tensor_tensor(w_lo[s][:], raw[s][:], w_hi[s][:], ALU.subtract).then_inc(w_lo_done[s], 1)


def shape_constants():
    c = np.zeros((P, C_COLS), np.float32)
    row, col = np.arange(P)[:, None], np.arange(P)[None, :]
    c[:, C_IDENT:C_IDENT + P] = row == col
    c[:, C_NEG_ONES:C_NEG_ONES + P] = -1.0
    c[:, C_NEG_TRI:C_NEG_TRI + P] = -1.0 * (row >= col)
    c[:, C_PAST:C_PAST + P] = row < col
    c[:, C_NOT_PAST:C_NOT_PAST + P] = np.where(row < col, 0.0, -1e30)
    c[:, C_CAUSAL:C_CAUSAL + P] = np.where(col <= row, 0.0, -1e30)
    half = ROPE // 2
    inv = np.float32(10000.0) ** (-np.arange(0, ROPE, 2, dtype=np.float32) / np.float32(ROPE))
    ang = (np.arange(S, dtype=np.float32)[None, :] * inv.astype(np.float32)[:, None]).astype(np.float32)
    r = np.zeros((2 * ROPE, S), np.float32)
    r[0:half] = r[half:ROPE] = np.cos(ang)
    r[ROPE:ROPE + half] = -np.sin(ang)
    r[ROPE + half:] = np.sin(ang)
    return c, r


INPUTS = ("x", "ln_g", "ln_b", "ffn_w_gate", "ffn_w_up", "ffn_w_down", "mix_w_in", "mla_q_norm_g", "mla_w_uq",
          "mla_kv_norm_g", "mla_w_ukv", "mix_w_out", "conv_w_in", "conv_w", "conv_w_out")


def kernel(**inputs):
    from concourse import bacc
    from concourse.bass_utils import run_bass_kernel_spmd

    nc = bacc.Bacc("TRN2", target_bir_lowering=False, num_devices=1)
    arrays = {name: np.ascontiguousarray(inputs[name]) for name in INPUTS}
    arrays["shape_consts"], arrays["rope_tables"] = shape_constants()
    args = [nc.dram_tensor(n, a.shape, mybir.dt.from_np(a.dtype), kind="ExternalInput").ap() for n, a in arrays.items()]
    args.append(nc.dram_tensor("trunk_out", (1, S, D), F32, kind="ExternalOutput").ap())
    build_trunk(nc, *args)
    result = run_bass_kernel_spmd(nc, [arrays], core_ids=[0])
    return result.results[0]["trunk_out"]
```

```python
from contextlib import ExitStack

import numpy as np

import concourse.bass as bass
from concourse import mybir

F32 = mybir.dt.float32
F32R = mybir.dt.float32r
ALU = mybir.AluOpType
ACT = mybir.ActivationFunctionType
AX = mybir.AxisListType

P = 128
S = 512
D = 1024
F = 2816
KT = D // P
TT = S // P
FT = F // P
PAIRS = FT // 2
UNIT = KT * 2 * P
HALF = D // 2
ALPHA = 4.0 ** 0.25
LN_EPS = 1e-5
RMS_EPS = 1e-6

SB_W = 512
HD = 64
ROPE = 32
Q_RANK = 768
KV_RANK = 256
MLA_HEAD_Q = HD + ROPE
MLA_SCALE = float(MLA_HEAD_Q) ** -0.5
HEAD_PAIRS = 4
LATENT_UNITS = (Q_RANK + KV_RANK) // 256
DOWN_UNITS = F // 256
FFN_TAIL = (2, 0, 1)
MIX_TAIL = (1, 2, 0)

STAGES = (("ffn", 0, 0), ("attn", 0, 1), ("ffn", 0, 2), ("ffn", 1, 0), ("conv", 1, 1), ("ffn", 1, 2))

SLOT_UNITS = {"ffn": (16, 16, 1), "conv": (6, 5, 5), "attn": (12, 11, 2)}
SLOT_DMAS = {"ffn": (16, 16, 1), "conv": (6, 5, 5), "attn": (16, 11, 2)}
LEFT_UNITS = {"ffn": (5, 5, 1), "conv": (2, 1, 1), "attn": (2, 1, 1)}
DOWN_USED = {"ffn": 10, "conv": 3, "attn": 3}

C_IDENT, C_NEG_ONES, C_PAST, C_CAUSAL, C_KEPT, C_NEG_TRI, C_NOT_PAST, C_COLS = 0, 128, 256, 384, 512, 512, 640, 768
ROWS_TAPS, ROWS_QG, ROWS_KVG, N_ROWS = 0, 24, 30, 32


def build_trunk(nc, x, ln_g, ln_b, w_gate, w_up, w_down, mix_in, q_norm_g, w_uq, kv_norm_g, w_ukv,
                mix_out, conv_in, conv_w, conv_out, consts, rope, out, stages=STAGES):
    n_stages = len(stages)

    def before(table, k, s=None):
        return sum(table[kind][s] if s is not None else table[kind] for kind, _, _ in stages[:k])

    def ffns_before(k):
        return sum(kind == "ffn" for kind, _, _ in stages[:k])

    with ExitStack() as ctx:
        def sb(name, shape, dt):
            return ctx.enter_context(nc.sbuf_tensor(name, shape, dt))

        def sem(name):
            return ctx.enter_context(nc.semaphore(name))

        raw = [sb(f"raw{s}", [P, UNIT], F32) for s in range(3)]
        w_hi = [sb(f"w_hi{s}", [P, UNIT], F32R) for s in range(3)]
        w_lo = [sb(f"w_lo{s}", [P, UNIT], F32R) for s in range(3)]
        left_hi = [sb(f"left_hi{s}", [P, 2, S], F32R) for s in range(3)]
        left_lo = [sb(f"left_lo{s}", [P, 2, S], F32R) for s in range(3)]
        xn = sb("xn", [P, TT, D], F32)
        xT_hi = sb("xT_hi", [P, KT, S], F32R)
        xT_lo = sb("xT_lo", [P, KT, S], F32R)
        h = sb("h", [P, FT, S], F32)
        gb = sb("gb", [P, 2, D], F32)
        gs = sb("gs", [P, 2, S], F32)
        cst = sb("cst", [P, C_KEPT], F32)
        rows = sb("rows", [N_ROWS, P], F32)
        cols = sb("cols", [P, N_ROWS], F32)
        stats = sb("stats", [P, 2, 6], F32)
        mean_var = sb("mean_var", [P, 2], F32)
        neg_max = sb("neg_max", [P, TT], F32)
        p_sum = sb("p_sum", [P, TT], F32)
        veps = sb("veps", [P, 1], F32)
        rstd = sb("rstd", [P, TT], F32)
        half_neg = sb("half_neg", [P, 1], F32)
        taps = sb("taps", [P, 3, 2], F32)
        rope_sb = sb("rope_sb", [P, S], F32)
        ident_r = sb("ident_r", [P, P], F32R)
        tri_r = sb("tri_r", [P, 2 * P], F32R)
        not_past_r = sb("not_past_r", [P, P], F32R)
        rms_eps = sb("rms_eps", [P, 2], F32)
        ps = ctx.enter_context(nc.psum_tensor("ps", [P, 8, 512], F32))

        ident = cst[:, C_IDENT:C_IDENT + P]
        mask_source = h[:, FT - 1, 0:C_COLS - C_KEPT]

        x_in = [sem(f"x_in{t}") for t in range(TT)]
        ident_in = sem("ident_in")
        consts_in = sem("consts_in")
        raw_full = [sem(f"raw_full{s}") for s in range(3)]
        gb_full = sem("gb_full")
        out_stored = sem("out_stored")
        w_hi_done = [sem(f"w_hi_done{s}") for s in range(3)]
        w_lo_done = [sem(f"w_lo_done{s}") for s in range(3)]
        left_hi_done = [sem(f"left_hi_done{s}") for s in range(3)]
        left_lo_done = [sem(f"left_lo_done{s}") for s in range(3)]
        down_used = sem("down_used")
        gate_done = sem("gate_done")
        up_done = sem("up_done")
        silu_done = sem("silu_done")
        h_done = sem("h_done")
        conv_c_done = sem("conv_c_done")
        conv_h_done = sem("conv_h_done")
        conv_b_done = sem("conv_b_done")
        c_copied = sem("c_copied")
        u_done = sem("u_done")
        conv_step = sem("conv_step")
        conv_out_done = sem("conv_out_done")
        u_zeroed = sem("u_zeroed")
        taps_set = sem("taps_set")
        lat_done = sem("lat_done")
        lat_squared = sem("lat_squared")
        sums_zeroed = sem("sums_zeroed")
        sq_added = sem("sq_added")
        sum_done = sem("sum_done")
        mean_root = sem("mean_root")
        rms_ready = sem("rms_ready")
        lat_scaled = sem("lat_scaled")
        lat_hi_done = sem("lat_hi_done")
        lat_ready = sem("lat_ready")
        kr_done = sem("kr_done")
        kr_step = sem("kr_step")
        masks_ready = sem("masks_ready")
        sbq_done = sem("sbq_done")
        sbk_done = sem("sbk_done")
        sbv_done = sem("sbv_done")
        sbq_hi_done = sem("sbq_hi_done")
        sbk_hi_done = sem("sbk_hi_done")
        sbq_ready = sem("sbq_ready")
        sbk_ready = sem("sbk_ready")
        sb_vT_copied = sem("sb_vT_copied")
        sb_v_turned = sem("sb_v_turned")
        sb_v_ready = sem("sb_v_ready")
        z_done = sem("z_done")
        soft_step = sem("soft_step")
        log_ready = sem("log_ready")
        keep_step = sem("keep_step")
        keep_ready = sem("keep_ready")
        stick_hi_done = sem("stick_hi_done")
        stick_ready = sem("stick_ready")
        stick_done = sem("stick_done")
        sb_w_done = sem("sb_w_done")
        sb_pv_done = sem("sb_pv_done")
        sb_oA_copied = sem("sb_oA_copied")
        sb_oB_copied = sem("sb_oB_copied")
        mq_done = sem("mq_done")
        mk_done = sem("mk_done")
        mv_done = sem("mv_done")
        mq_step = sem("mq_step")
        mq_nope_copied = sem("mq_nope_copied")
        mq_rope_ready = sem("mq_rope_ready")
        mk_copied = sem("mk_copied")
        k_rope_placed = sem("k_rope_placed")
        mvT_copied = sem("mvT_copied")
        mv_turned = sem("mv_turned")
        mv_ready = sem("mv_ready")
        s_done = sem("s_done")
        max_step = sem("max_step")
        max_ready = sem("max_ready")
        exp_done = sem("exp_done")
        norm_step = sem("norm_step")
        p_ready = sem("p_ready")
        p_turned = sem("p_turned")
        pT_copied = sem("pT_copied")
        mla_pv_done = sem("mla_pv_done")
        mla_oA_copied = sem("mla_oA_copied")
        mla_oB_copied = sem("mla_oB_copied")
        y_done = sem("y_done")
        ln_step = sem("ln_step")
        var_ready = sem("var_ready")
        rstd_ready = sem("rstd_ready")
        x_done = sem("x_done")
        turned = sem("turned")
        xT_hi_done = sem("xT_hi_done")
        xT_ready = sem("xT_ready")
        res_ready = sem("res_ready")
        rows_turned = sem("rows_turned")
        cols_ready = sem("cols_ready")
        exp_ready = sem("exp_ready")

        h_flat = h[:].rearrange("p f s -> p (f s)")
        U_PAD = 2
        U_W = S + 4
        conv_u = [h_flat[:, KT * S + c * U_W:KT * S + (c + 1) * U_W] for c in range(2)]
        conv_acc = [h[:, KT + 4 + c, :] for c in range(2)]

        latent = [h[:, KT + ct, :] for ct in range(KT)]
        pT = [h[:, KT + 4 * a:KT + 4 * a + 4, :] for a in range(2)]
        scratch = [raw[2][:, n * S:(n + 1) * S] for n in range(4)]
        k_rope, sq_sum, rope_tmp, mla_vT = scratch[0], scratch[1:3], scratch[3], scratch[0]
        sbq = (left_hi[0][:, 0, :], left_lo[0][:, 0, :])
        sbk = (left_hi[0][:, 1, :], left_lo[0][:, 1, :])
        sb_vT, sb_v = gs[:, 0, :], gs[:, 1, :].rearrange("p (k n) -> p k n", k=TT)
        Z_W = sum(S - P * i for i in range(TT))
        Z_AT = (0, 512, 1024, 896)
        stick = [h_flat[:, 2 * KT * S + a * Z_W:2 * KT * S + (a + 1) * Z_W] for a in range(2)]
        ps_flat = ps[:].rearrange("p b n -> p (b n)")
        z = [ps_flat[:, 1536 * a:1536 * a + Z_W] for a in range(2)]
        stick_hi = [w[2][:, 0:Z_W] for w in (w_hi, w_lo)]

        def stick_lo(a, i):
            w = (w_hi, w_lo)[a]
            if i == 2:
                return w[2][:, Z_W:Z_W + S - 2 * P]
            return w[1][:, KT * P + Z_AT[i]:KT * P + Z_AT[i] + S - P * i]

        mq = [gs[:, 0, :], scratch[2]]
        mk = [h[:, 21, :], scratch[1]]
        mv = gs[:, 1, :].rearrange("p (k n) -> p k n", k=TT)
        prob = [h[:, 16 + t, :] for t in range(TT)]

        def kv_view(w, part):
            return w[:, 0:2 * 256].rearrange("p (k c a n) -> p k c a n", k=2, c=2, a=2)[:, :, part, :, :]

        def kv_raw(part):
            return raw[1][:, 0:2 * 256].rearrange("p (k a c n) -> p k a c n", k=2, a=2, c=2)[:, :, :, part, :]

        LAT_BANK = (0, 1, 2, 3, 5, 6, 7, 0)
        up_view = [(w_hi[s][:].rearrange("p (k n) -> p k n", k=KT), w_lo[s][:].rearrange("p (k n) -> p k n", k=KT))
                   for s in range(3)]
        down_view = [(w_hi[s][:].rearrange("p (f n) -> p f n", f=2), w_lo[s][:].rearrange("p (f n) -> p f n", f=2))
                     for s in range(3)]

        def col_units(w, col):
            return w.rearrange("(k p) n -> p k n", p=P)[:, :, bass.ds(col, 256)]

        def row_units(w, u):
            return w[bass.ds(u * 256, 256), :].rearrange("(f p) n -> p f n", p=P)

        block = ctx.enter_context(nc.Block())

        @block.sync
        def _(sp):
            def load(s, src, k, n):
                free = before(SLOT_UNITS, k, s) + n
                if not isinstance(free, int) or free > 0:
                    sp.wait_ge(w_lo_done[s], free)
                sp.dma_start(raw[s][:].rearrange("p (a n) -> p a n", a=src.shape[1]), src).then_inc(raw_full[s], 16)

            def first_units(k, slots=(0, 1)):
                kind, layer, idx = stages[k]
                units = {"ffn": lambda: (col_units(w_gate[layer, idx // 2], 0), col_units(w_up[layer, idx // 2], 0)),
                         "conv": lambda: (col_units(conv_in[0], D), col_units(conv_in[0], 2 * D)),
                         "attn": lambda: (col_units(mix_in[0], 3 * SB_W), col_units(mix_in[0], 3 * SB_W + 256))}[kind]()
                for s in slots:
                    load(s, units[s], k, 0)

            def sb_col(p, n):
                at = p * P + n * SB_W
                return at if isinstance(at, int) else sp.snap(at)

            def sb_units(k, p):
                view = mix_in[0].rearrange("(k p) n -> p k n", p=P)
                sp.wait_ge(w_lo_done[0], p + (before(SLOT_UNITS, k, 0) + 2))
                for n in range(2):
                    sp.dma_start(raw[0][:].rearrange("p (k n) -> p k n", k=KT)[:, :, n * P:(n + 1) * P],
                                 view[:, :, bass.ds(sb_col(p, n), P)]).then_inc(raw_full[0], 16)
                at = sb_col(p, 2)
                sp.wait_ge(w_lo_done[1], p + (before(SLOT_UNITS, k, 1) + 2))
                sp.dma_start(raw[1][:, 0:KT * P].rearrange("p (k n) -> p k n", k=KT),
                             view[:, :, bass.ds(at, P)]).then_inc(raw_full[1], 16)

            def mla_units(k, p):
                sp.wait_ge(w_lo_done[0], p + (before(SLOT_UNITS, k, 0) + 6))
                sp.dma_start(raw[0][:, 0:6 * 192].rearrange("p (k n) -> p k n", k=6),
                             w_uq[0].rearrange("(k p) n -> p k n", p=P)[:, :, bass.ds(p * 192, 192)]).then_inc(raw_full[0], 16)
                at = sp.snap(p * 256) if not isinstance(p, int) else p * 256
                sp.wait_ge(w_lo_done[1], p + (before(SLOT_UNITS, k, 1) + 6))
                sp.dma_start(raw[1][:, 0:2 * 256].rearrange("p (k n) -> p k n", k=2),
                             w_ukv[0].rearrange("(k p) n -> p k n", p=P)[:, :, bass.ds(at, 256)]).then_inc(raw_full[1], 16)

            def load_x(t):
                sp.dma_start(xn[:, t, :], x[0, t * P:(t + 1) * P, :]).then_inc(x_in[t], 16)

            sp.dma_start(ident, consts[:, C_IDENT:C_IDENT + P]).then_inc(ident_in, 16)
            load_x(0)
            load_x(1)
            first_units(0, (0,))
            load_x(2)
            first_units(0, (1,))
            load_x(3)
            sp.dma_start(cst[:, P:], consts[:, P:C_KEPT]).then_inc(consts_in, 16)
            sp.dma_start(mask_source, consts[:, C_KEPT:]).then_inc(consts_in, 16)
            sp.dma_start(rope_sb[HD:P, :], rope).then_inc(consts_in, 16)
            sp.dma_start(rows[ROWS_TAPS:ROWS_QG, :], conv_w[0].rearrange("k (c p) -> (k c) p", p=P)).then_inc(consts_in, 16)
            sp.dma_start(rows[ROWS_QG:ROWS_KVG, :], q_norm_g[0].rearrange("(c p) -> c p", p=P)).then_inc(consts_in, 16)
            sp.dma_start(rows[ROWS_KVG:N_ROWS, :], kv_norm_g[0].rearrange("(c p) -> c p", p=P)).then_inc(consts_in, 16)
            for k, (kind, layer, idx) in enumerate(stages):
                if kind == "ffn":
                    j = idx // 2
                    load(2, row_units(w_down[layer, j], DOWN_UNITS - 1), k, 0)
                    with sp.Fori(1, PAIRS) as i:
                        load(0, col_units(w_gate[layer, j], i * 256), k, i)
                        load(1, col_units(w_up[layer, j], i * 256), k, i)
                    with sp.Fori(0, (DOWN_UNITS - 1) // 2) as i:
                        load(0, row_units(w_down[layer, j], i * 2), k, i + PAIRS)
                        load(1, row_units(w_down[layer, j], i * 2 + 1), k, i + PAIRS)
                if kind == "conv":
                    load(2, col_units(conv_in[0], 0), k, 0)
                    with sp.Fori(0, KT // 2 - 1) as i:
                        load(0, col_units(conv_in[0], i * 256 + (D + 256)), k, i + 1)
                        load(1, col_units(conv_in[0], i * 256 + (2 * D + 256)), k, i + 1)
                        load(2, col_units(conv_in[0], i * 256 + 256), k, i + 1)
                    for u, (s, n) in enumerate(((0, 4), (1, 4), (2, 4), (0, 5))):
                        load(s, row_units(conv_out[0], u), k, n)
                if kind == "attn":
                    w0, w1, w2 = (before(SLOT_UNITS, k, s) for s in range(3))
                    if w2:
                        sp.wait_ge(w_lo_done[2], w2)
                    sp.dma_start(raw[2][:, 0:KT * ROPE].rearrange("p (k n) -> p k n", k=KT),
                                 mix_in[0].rearrange("(k p) n -> p k n", p=P)[:, :, 3 * SB_W + D:]).then_inc(raw_full[2], 16)
                    load(0, col_units(mix_in[0], 3 * SB_W + 512), k, 1)
                    load(1, col_units(mix_in[0], 3 * SB_W + 768), k, 1)
                    with sp.Fori(0, HEAD_PAIRS) as p:
                        sb_units(k, p)
                    with sp.Fori(0, HEAD_PAIRS) as p:
                        mla_units(k, p)
                    load(0, row_units(mix_out[0], 0), k, 10)
                    load(1, row_units(mix_out[0], 1), k, 10)
                    sp.wait_ge(s_done, 8 * HEAD_PAIRS)
                    sp.wait_ge(mv_ready, HEAD_PAIRS)
                    load(2, row_units(mix_out[0], 2), k, 1)
                    load(0, row_units(mix_out[0], 3), k, 11)
                if k + 1 < n_stages:
                    first_units(k + 1)
            for t in range(TT):
                parts = 2 if t == TT - 1 else 1
                for n in range(parts):
                    cut = slice(n * D // parts, (n + 1) * D // parts)
                    sp.wait_ge(x_done, TT * (n_stages - 1) + t + n + 1)
                    sp.dma_start(out[0, t * P:(t + 1) * P, cut], xn[:, t, cut]).then_inc(out_stored, 16)
            sp.wait_ge(out_stored, 16 * (TT + 1))

        @block.tensor
        def _(pe):
            def product3(dst, left, right, first, last):
                pe.matmul(dst, left[0], right[0], start=first, stop=False)
                pe.matmul(dst, left[0], right[1], start=False, stop=False)
                return pe.matmul(dst, left[1], right[0], start=False, stop=last)

            def project_up(bank, s, c):
                hi, lo = up_view[s]
                for kt in range(KT):
                    mm = product3(ps[:, bank, :], (hi[:, kt, c * P:(c + 1) * P], lo[:, kt, c * P:(c + 1) * P]),
                                  (xT_hi[:, kt, :], xT_lo[:, kt, :]), kt == 0, kt == KT - 1)
                return mm

            def project_tokens(bank, s, c, t0, t1):
                hi, lo = up_view[s]
                cut = slice(t0 * P, t1 * P)
                for kt in range(KT):
                    left = [w[:, kt, c * P:(c + 1) * P] for w in (hi, lo)]
                    for n, (a, b) in enumerate(((0, xT_hi), (0, xT_lo), (1, xT_hi))):
                        mm = pe.matmul(ps[:, bank, cut], left[a], b[:, kt, cut], start=t0 == kt == n == 0,
                                       stop=kt == KT - 1 and n == 2, skip_group_check=True)
                return mm

            def head(k, done0, done1):
                pe.wait_ge(xT_ready, 8 * k + 4)
                pe.wait_ge(w_lo_done[0], before(SLOT_UNITS, k, 0) + 1)
                for c in range(2):
                    project_tokens(c, 0, c, 0, 2)
                turn(k, 3)
                pe.wait_ge(w_lo_done[1], before(SLOT_UNITS, k, 1) + 1)
                for c in range(2):
                    project_tokens(2 + c, 1, c, 0, 2)
                pe.wait_ge(xT_ready, 8 * k + 8)
                for c in range(2):
                    project_tokens(c, 0, c, 2, 4).then_inc(done0, 1)
                for c in range(2):
                    project_tokens(2 + c, 1, c, 2, 4).then_inc(done1, 1)

            def project_down(t, half, s, f, first, last):
                hi, lo = down_view[s]
                return product3(ps[:, 2 * t + half, :],
                                (left_hi[s][:, f, t * P:(t + 1) * P], left_lo[s][:, f, t * P:(t + 1) * P]),
                                (hi[:, f, half * HALF:(half + 1) * HALF], lo[:, f, half * HALF:(half + 1) * HALF]),
                                first, last)

            def wait_down_unit(k, s, w_n, left_n):
                pe.wait_ge(w_lo_done[s], w_n + (before(SLOT_UNITS, k, s) + 1))
                pe.wait_ge(left_lo_done[s], left_n + (before(LEFT_UNITS, k, s) + 1))

            def down_early(k, t):
                for half in range(1 if t == 3 else 0, 2):
                    if t < 2:
                        pe.wait_ge(exp_done, 8 * (HEAD_PAIRS - 1) + 4 + 2 * t + half + 1)
                    for s in range(2):
                        wait_down_unit(k, s, 10, 0)
                        for f in range(2):
                            project_down(t, half, s, f, s == f == 0, False)

            def down_unit(k, s, order, first=False):
                for t in order:
                    if first and stages[k][0] == "conv" and t < 3:
                        read, n = ((c_copied, KT), (u_done, KT), (conv_out_done, KT))[t]
                        pe.wait_ge(read, n + 2)
                    if first and t == 0 and stages[k][0] == "ffn":
                        pe.wait_ge(h_done, FT * (ffns_before(k) + 1) + 2)
                    if first and t == 3 and k == 0:
                        pe.wait_ge(cols_ready, 1)
                    for half in range(2):
                        for f in range(2):
                            mm = project_down(t, half, s, f, first and f == 0, False)
                mm.then_inc(down_used, 1)

            def sb_query(k, n):
                pe.wait_ge(w_lo_done[0], n + (before(SLOT_UNITS, k, 0) + 3))
                project_up(6, 0, 0).then_inc(sbq_done, 1)

            def sb_key(n):
                project_up(7, 0, 1).then_inc(sbk_done, 1)

            def sb_value(k, n):
                pe.wait_ge(w_lo_done[1], n + (before(SLOT_UNITS, k, 1) + 3))
                pe.wait_ge(sbq_ready, n + 1)
                hi, lo = (w[1][:, 0:KT * P].rearrange("p (k n) -> p k n", k=KT) for w in (w_hi, w_lo))
                for kt in range(KT):
                    mm = product3(ps[:, 6, :], (hi[:, kt, :], lo[:, kt, :]), (xT_hi[:, kt, :], xT_lo[:, kt, :]),
                                  kt == 0, kt == KT - 1)
                mm.then_inc(sbv_done, 1)

            def sb_value_turn(n):
                pe.wait_ge(sb_vT_copied, n + 1)
                for t in range(TT):
                    mm = pe.transpose(ps[:, 5, t * P:(t + 1) * P], sb_vT[:, t * P:(t + 1) * P], ident)
                mm.then_inc(sb_v_turned, 1)

            def sb_pair(k, p, last):
                for a in range(2):
                    rows_a = slice(HD * a, HD * a + HD)
                    if a == 0:
                        pe.wait_ge(sbk_ready, p + 1)
                        pe.wait_ge(sbq_ready, p + 1)
                    else:
                        pe.wait_ge(sb_v_ready, p + 1)
                    for i in range(TT):
                        at, w = Z_AT[i], S - P * i
                        left = [t[rows_a, i * P:(i + 1) * P] for t in sbk]
                        right = [t[rows_a, i * P:S] for t in sbq]
                        dst = z[a][:, at:at + w]
                        pe.matmul(dst, left[0], right[0], start=i < 3, stop=False, skip_group_check=True)
                        pe.matmul(dst, left[0], right[1], start=False, stop=False, skip_group_check=True)
                        mm = pe.matmul(dst, left[1], right[0], start=False, stop=False, skip_group_check=True)
                    mm.then_inc(z_done, 1)
                pe.wait_ge(sb_oB_copied, p + 1)
                if last:
                    pe.wait_ge(lat_ready, KT)
                    mla_query(k, 0, 0)
                else:
                    sb_query(k, p + 1)
                pe.wait_ge(sb_oA_copied, p + 1)
                if last:
                    mla_query(k, 0, 1)
                else:
                    sb_key(p + 1)
                for a in range(2):
                    pe.wait_ge(stick_ready, p * 2 + (a + 1))
                    for i in range(TT):
                        at, w = Z_AT[i], S - P * i
                        pe.matmul(z[a][:, at:at + P], ident_r[:], not_past_r[:], start=False, stop=False,
                                  skip_group_check=True)
                        for j in range(i, TT):
                            ones = tri_r[:, P:2 * P] if j == i else tri_r[:, 0:P]
                            dst = z[a][:, at + P * (j - i):at + w]
                            pe.matmul(dst, ones, stick_hi[a][:, Z_AT[j]:Z_AT[j] + S - P * j], start=False,
                                      stop=False, skip_group_check=True)
                            mm = pe.matmul(dst, ones, stick_lo(a, j), start=False, stop=j == TT - 1,
                                           skip_group_check=True)
                    mm.then_inc(stick_done, 1)
                    if a == 0 and last:
                        mla_key(k, 0)
                    elif a == 0:
                        sb_value(k, p + 1)
                for a in range(2):
                    pe.wait_ge(sb_w_done, p * 2 + (a + 1))
                    if last:
                        if a == 1:
                            mla_kv(k, 0, 1, mv_done, 5)
                        pe.wait_ge(*(mk_copied, 2) if a else (mq_nope_copied, 2))
                        if a == 0:
                            pe.wait_ge(mq_rope_ready, 2)
                    else:
                        pe.wait_ge((sbk_ready, sb_vT_copied)[a], p + 2)
                    for i in range(TT):
                        mm = pe.matmul(ps[:, 7 - a, i * P:S], sb_v[:, i, :], stick[a][:, Z_AT[i]:Z_AT[i] + S - P * i],
                                       start=i == 0, stop=i == TT - 1)
                    mm.then_inc(sb_pv_done, 1)
                if last:
                    mla_value_turn(0)
                else:
                    sb_value_turn(p + 1)

            def mla_query(k, n, a):
                pe.wait_ge(w_lo_done[0], n + (before(SLOT_UNITS, k, 0) + 7))
                hi, lo = (w[0][:, 0:6 * 256].rearrange("p (k n) -> p k n", k=6) for w in (w_hi, w_lo))
                for kt in range(6):
                    mm = product3(ps[:, 6 + a, :], (hi[:, kt, a * P:(a + 1) * P], lo[:, kt, a * P:(a + 1) * P]),
                                  (xT_hi[:, kt, :], xT_lo[:, kt, :]), kt == 0, kt == 5)
                mm.then_inc(mq_done, 1)

            def mla_kv(k, n, part, done, bank=6):
                pe.wait_ge(w_lo_done[1], n + (before(SLOT_UNITS, k, 1) + 7))
                hi, lo = (w[1][:, 0:2 * 256].rearrange("p (k c n) -> p k c n", k=2, c=2) for w in (w_hi, w_lo))
                for kt in range(2):
                    mm = product3(ps[:, bank, :], (hi[:, kt, part, :], lo[:, kt, part, :]),
                                  (xT_hi[:, 6 + kt, :], xT_lo[:, 6 + kt, :]), kt == 0, kt == 1)
                mm.then_inc(done, 1)

            def mla_key(k, n):
                pe.wait_ge(mq_rope_ready, n * 2 + 1)
                pe.wait_ge(mq_nope_copied, n * 2 + 1)
                mla_kv(k, n, 0, mk_done)

            def mla_value_turn(n):
                pe.wait_ge(mvT_copied, n + 1)
                for t in range(TT):
                    mm = pe.transpose(ps[:, 3, t * P:(t + 1) * P], mla_vT[:, t * P:(t + 1) * P], ident)
                mm.then_inc(mv_turned, 1)

            def mla_scores(p, a, t):
                if a == 1:
                    pe.wait_ge(exp_done, p * 8 + (t + 1))
                if t == 0:
                    pe.wait_ge(mq_rope_ready, p * 2 + (a + 1))
                    pe.wait_ge(mq_nope_copied, p * 2 + (a + 1))
                    pe.wait_ge(mk_copied, p * 2 + (a + 1))
                if a == 0 and t == 3:
                    pe.wait_ge(mv_ready, p + 1)
                keys = P * (t + 1)
                pe.matmul(ps[:, t, 0:keys], mq[a][0:MLA_HEAD_Q, t * P:(t + 1) * P], mk[a][0:MLA_HEAD_Q, 0:keys],
                          start=True, stop=True).then_inc(s_done, 1)

            def mla_turn(p, a, t):
                n = 4 * a + t
                pe.wait_ge(p_ready, p * 8 + (n + 1))
                if n >= 2:
                    pe.wait_ge(pT_copied, p * 8 + (n - 1))
                for kt in range(t + 1):
                    mm = pe.transpose(ps[:, 4 + n % 2, kt * P:(kt + 1) * P], prob[t][:, kt * P:(kt + 1) * P], ident)
                mm.then_inc(p_turned, 1)

            def mla_mix(p, a, bank=6):
                pe.wait_ge(pT_copied, p * 8 + 4 * (a + 1))
                for kt in range(TT):
                    mm = pe.matmul(ps[:, bank, kt * P:S], mv[:, kt, :], pT[a][:, kt, kt * P:S],
                                   start=kt == 0, stop=kt == TT - 1)
                mm.then_inc(mla_pv_done, 1)

            def mla_pair(k, p, more):
                for t in range(TT):
                    mla_scores(p, 0, t)
                pe.wait_ge(mla_oB_copied, p + 1)
                if more:
                    mla_query(k, p + 1, 0)
                else:
                    down_early(k, 3)
                mla_turn(p, 0, 0)
                mla_turn(p, 0, 1)
                mla_scores(p, 1, 0)
                mla_scores(p, 1, 1)
                mla_turn(p, 0, 2)
                mla_turn(p, 0, 3)
                mla_scores(p, 1, 2)
                mla_scores(p, 1, 3)
                if more:
                    mla_query(k, p + 1, 1)
                else:
                    down_early(k, 0)
                mla_turn(p, 1, 0)
                mla_turn(p, 1, 1)
                if more:
                    mla_key(k, p + 1)
                else:
                    down_early(k, 1)
                mla_turn(p, 1, 2)
                mla_turn(p, 1, 3)
                if more:
                    pe.wait_ge(mk_copied, p * 2 + 4)
                mla_mix(p, 0)
                if more:
                    pe.wait_ge(mq_rope_ready, p * 2 + 4)
                    pe.wait_ge(mq_nope_copied, p * 2 + 4)
                    mla_kv(k, p + 1, 1, mv_done, 7)
                    pe.wait_ge(mla_oA_copied, p + 1)
                    mla_mix(p, 1)
                else:
                    mla_mix(p, 1, 4)
                if more:
                    mla_value_turn(p + 1)

            def latents(k):
                head(k, lat_done, lat_done)
                pe.wait_ge(w_lo_done[2], before(SLOT_UNITS, k, 2) + 1)
                hi, lo = (w[2][:, 0:KT * P].rearrange("p (k n) -> p k n", k=KT) for w in (w_hi, w_lo))
                for kt in range(KT):
                    mm = product3(ps[:, 4, :], (hi[:, kt, :], lo[:, kt, :]), (xT_hi[:, kt, :], xT_lo[:, kt, :]),
                                  kt == 0, kt == KT - 1)
                mm.then_inc(kr_done, 1)
                for u in range(2, LATENT_UNITS):
                    pe.wait_ge(w_lo_done[u % 2], before(SLOT_UNITS, k, u % 2) + u // 2 + 1)
                    for c in range(2):
                        ct = 2 * u + c
                        if ct == 7:
                            pe.wait_ge(lat_squared, 1)
                        project_up(LAT_BANK[ct], u % 2, c).then_inc(lat_done, 1)

            def latent_sum(n):
                pe.wait_ge(sq_added, (6, KT)[n])
                pe.matmul(ps[:, 1 + n, :], cst[:, C_NEG_ONES:C_NEG_ONES + P], sq_sum[n],
                          start=True, stop=True).then_inc(sum_done, 1)

            def turn(m, t):
                if m == 0:
                    pe.wait_ge(x_in[t], 16)
                else:
                    pe.wait_ge(x_done, TT * (m - 1) + t + 1)
                for kt in range(KT):
                    mm = pe.transpose(ps[:, 2 * t + kt // 4, (kt % 4) * P:(kt % 4 + 1) * P],
                                      xn[:, t, kt * P:(kt + 1) * P], ident)
                    if kt % 4 == 3:
                        mm.then_inc(turned, 1)

            def tail(k, order, w_n, left_n, early=()):
                more = k + 1 < n_stages

                def part(t, s, halves=(0, 1)):
                    for half in halves:
                        if s == 1 and (t, half) in early:
                            continue
                        for f in range(2):
                            mm = project_down(t, half, s, f, False, s == last and f == 1)
                        if s == last:
                            mm.then_inc(y_done, 1)
                    return mm

                last = order[2]
                steps = ((0, order[0]), (0, order[1]), (1, order[0]), (0, last), (1, order[1]), (1, last))
                if early:
                    steps = ((0, order[1]), (1, order[1]), (0, last), (1, last))
                for t, s in steps:
                    if t == 0:
                        wait_down_unit(k, s, w_n[s], left_n[s])
                    part(t, s)
                for half in range(2):
                    for s in order:
                        part(2, s, (half,))
                    if more:
                        turn(k + 1, half)
                last = 2
                for s in range(3):
                    mm = part(3, s)
                    if s < 2:
                        mm.then_inc(down_used, 1)
                if more:
                    turn(k + 1, 2)

            pe.wait_ge(ident_in, 16)
            for t in range(3):
                turn(0, t)

            for k, (kind, layer, idx) in enumerate(stages):
                w0, w1, w2 = (before(SLOT_UNITS, k, s) for s in range(3))
                if kind == "ffn":
                    p0 = FT * ffns_before(k)
                    head(k, gate_done, up_done)
                    if k == 0:
                        pe.wait_ge(consts_in, 96)
                        pe.transpose(ps[:, 7, 0:N_ROWS], rows[:],
                                     cst[0:N_ROWS, C_IDENT:C_IDENT + N_ROWS]).then_inc(rows_turned, 1)
                    with pe.Fori(1, PAIRS) as i:
                        pe.wait_ge(w_lo_done[0], i + (w0 + 1))
                        for c in range(2):
                            pe.wait_ge(silu_done, i * 2 + (p0 + 1 + c))
                            project_up(c, 0, c).then_inc(gate_done, 1)
                        pe.wait_ge(w_lo_done[1], i + (w1 + 1))
                        for c in range(2):
                            pe.wait_ge(h_done, i * 2 + (p0 + 1 + c))
                            project_up(2 + c, 1, c).then_inc(up_done, 1)
                    for u in range(2):
                        wait_down_unit(k, u, PAIRS, 0)
                        down_unit(k, u, (2, 3, 0, 1), first=u == 0)
                    with pe.Fori(1, (DOWN_UNITS - 3) // 2) as i:
                        for s in range(2):
                            wait_down_unit(k, s, i + PAIRS, i)
                            down_unit(k, s, range(TT))
                    tail(k, FFN_TAIL, (15, 15, 0), (4, 4, 0))
                if kind == "conv":
                    head(k, conv_c_done, conv_h_done)
                    pe.wait_ge(w_lo_done[2], w2 + 1)
                    for c in range(2):
                        project_up(4 + c, 2, c).then_inc(conv_b_done, 1)
                    with pe.Fori(1, KT // 2) as i:
                        for s, (read, done) in enumerate(((c_copied, conv_c_done), (u_done, conv_h_done),
                                                          (conv_out_done, conv_b_done))):
                            pe.wait_ge(w_lo_done[s], i + (before(SLOT_UNITS, k, s) + 1))
                            for c in range(2):
                                pe.wait_ge(read, i * 2 + (1 + c))
                                project_up(2 * s + c, s, c).then_inc(done, 1)
                    wait_down_unit(k, 0, 4, 0)
                    down_unit(k, 0, (3, 0, 1, 2), first=True)
                    tail(k, MIX_TAIL, (5, 4, 4), (1, 0, 0))
                if kind == "attn":
                    latents(k)
                    pe.wait_ge(lat_squared, 6)
                    sb_query(k, 0)
                    pe.wait_ge(lat_squared, 7)
                    sb_key(0)
                    latent_sum(0)
                    sb_value(k, 0)
                    latent_sum(1)
                    sb_value_turn(0)
                    pe.wait_ge(masks_ready, 4)
                    pe.wait_ge(lat_squared, KT)
                    pe.wait_ge(kr_step, 3)
                    pe.wait_ge(mean_root, 2)
                    with pe.Fori(0, HEAD_PAIRS - 2) as p:
                        sb_pair(k, p, False)
                    sb_pair(k, HEAD_PAIRS - 2, False)
                    sb_pair(k, HEAD_PAIRS - 1, True)
                    pe.wait_ge(sb_oA_copied, HEAD_PAIRS + 1)
                    pe.wait_ge(sb_oB_copied, HEAD_PAIRS + 1)
                    with pe.Fori(0, HEAD_PAIRS - 1) as p:
                        mla_pair(k, p, True)
                    mla_pair(k, HEAD_PAIRS - 1, False)
                    wait_down_unit(k, 0, 10, 0)
                    for t, half in ((2, 1), (3, 0), (2, 0)):
                        if t == 3:
                            pe.wait_ge(mla_oA_copied, HEAD_PAIRS)
                        if (t, half) == (2, 0):
                            pe.wait_ge(mla_oB_copied, HEAD_PAIRS + 1)
                        for f in range(2):
                            mm = project_down(t, half, 0, f, f == 0, False)
                    mm.then_inc(down_used, 1)
                    tail(k, MIX_TAIL, (11, 10, 1), (1, 0, 0), early=((0, 0), (0, 1), (1, 0), (1, 1), (3, 1)))

        @block.scalar
        def _(act):
            def split_w(k, s, n, width=UNIT, dmas=None):
                arrived = n + (before(SLOT_DMAS, k, s) + 1) if dmas is None else dmas
                act.wait_ge(raw_full[s], arrived * 16)
                act.activation(w_hi[s][:, 0:width], raw[s][:, 0:width], ACT.Copy).then_inc(w_hi_done[s], 1)

            def split_left(s, f):
                act.activation(left_hi[s][:], h[:, bass.ds(f, 2), :], ACT.Copy).then_inc(left_hi_done[s], 1)

            def turn_hi(m, t):
                for half in range(2):
                    act.wait_ge(turned, 8 * m + 2 * t + half + 1)
                    act.activation(xT_hi[:, 4 * half:4 * half + 4, t * P:(t + 1) * P],
                                   ps[:, 2 * t + half, :].rearrange("p (k n) -> p k n", k=4),
                                   ACT.Copy).then_inc(xT_hi_done, 1)

            def close_stage(k):
                if k + 1 == n_stages:
                    return
                turn_hi(k + 1, 0)
                turn_hi(k + 1, 1)
                act.wait_ge(down_used, before(DOWN_USED, k + 1) - 1)
                split_w(k + 1, 0, 0)
                act.wait_ge(down_used, before(DOWN_USED, k + 1))
                split_w(k + 1, 1, 0)
                turn_hi(k + 1, 2)
                turn_hi(k + 1, 3)

            def rotary_views(dst, src, kts, heads, lead):
                half = ROPE // 2
                d = dst.rearrange("p (k a n) -> p k a n", k=kts, a=heads)
                r = src.rearrange("p (k a n) -> p k a n", k=kts, a=heads)
                return ((d[:, :, :, HD - lead:HD + ROPE], r),
                        (d[:, :, :, HD + ROPE:HD + ROPE + half], r[:, :, :, lead + half:lead + ROPE]),
                        (d[:, :, :, HD + ROPE + half:P], r[:, :, :, lead:lead + half]))

            def split_rotary(k, s, n, kts, heads, lead):
                act.wait_ge(raw_full[s], (n + (before(SLOT_DMAS, k, s) + 1)) * 16)
                for dst, src in rotary_views(w_hi[s][:, 0:kts * heads * P],
                                             raw[s][:, 0:kts * heads * (lead + ROPE)], kts, heads, lead):
                    last = act.activation(dst, src, ACT.Copy)
                last.then_inc(w_hi_done[s], 1)

            def split_kv(k, n):
                act.wait_ge(raw_full[1], (n + (before(SLOT_DMAS, k, 1) + 1)) * 16)
                for part in range(2):
                    last = act.activation(kv_view(w_hi[1], part), kv_raw(part), ACT.Copy)
                last.then_inc(w_hi_done[1], 1)

            def latent_tiles(k):
                for ct in range(KT):
                    act.wait_ge(lat_done, ct + 1)
                    act.activation(latent[ct], ps[:, LAT_BANK[ct], :], ACT.Copy)
                    if ct >= 2:
                        act.wait_ge(sq_added, ct - 1)
                    act.activation(gs[:, ct % 2, :], ps[:, LAT_BANK[ct], :], ACT.Square).then_inc(lat_squared, 1)
                    if ct == 1:
                        split_w(k, 0, 1)
                        split_rotary(k, 2, 0, KT, 1, 0)
                    if ct == 3:
                        split_w(k, 1, 1)
                    if ct == 5:
                        split_w(k, 0, 2, dmas=before(SLOT_DMAS, k, 0) + 4)
                split_w(k, 1, 2, width=KT * P)

            def split_sb(k, s, n):
                if s == 0:
                    act.wait_ge(raw_full[0], n * 32 + 16 * (before(SLOT_DMAS, k, 0) + 4))
                    act.activation(w_hi[0][:], raw[0][:], ACT.Copy).then_inc(w_hi_done[0], 1)
                else:
                    split_w(k, 1, n + 2, width=KT * P)

            def sb_query_hi(n):
                act.wait_ge(sbq_done, n + 1)
                act.activation(sbq[0], ps[:, 6, :], ACT.Copy, scale=HD ** -0.5).then_inc(sbq_hi_done, 1)

            def sb_key_hi(n):
                act.wait_ge(sbk_done, n + 1)
                act.activation(sbk[0], ps[:, 7, :], ACT.Copy).then_inc(sbk_hi_done, 1)

            def sb_value_copy(n):
                act.wait_ge(sbv_done, n + 1)
                act.activation(sb_vT, ps[:, 6, :], ACT.Copy).then_inc(sb_vT_copied, 1)

            def sb_pair(k, p, kind):
                last = kind == "last"
                for a in range(2):
                    act.wait_ge(z_done, p * 2 + (a + 1))
                    act.activation(stick[a], z[a], ACT.Abs).then_inc(soft_step, 1)
                    act.wait_ge(soft_step, p * 4 + (2 * a + 1))
                    act.activation(stick[a], stick[a], ACT.Exp, scale=-1.0).then_inc(soft_step, 1)
                    act.wait_ge(soft_step, p * 4 + (2 * a + 2))
                    act.activation(stick[a], stick[a], ACT.Ln, bias=1.0).then_inc(log_ready, 1)
                for a in range(2):
                    act.wait_ge(keep_ready, p * 2 + (a + 1))
                    act.activation(stick_hi[a], stick[a], ACT.Copy).then_inc(stick_hi_done, 1)
                    if last:
                        mla_query_copy(0, a)
                    else:
                        (sb_query_hi, sb_key_hi)[a](p + 1)
                if kind == "sb":
                    split_sb(k, 0, p + 2)
                if kind == "mla":
                    split_rotary(k, 0, 10, 6, 2, HD)
                act.wait_ge(stick_done, p * 2 + 1)
                act.activation(stick[0], z[0], ACT.Exp).then_inc(sb_w_done, 1)
                if last:
                    mla_key_copy(0)
                else:
                    sb_value_copy(p + 1)
                if kind == "mla":
                    latent_hi(0, 4)
                act.wait_ge(stick_done, p * 2 + 2)
                act.activation(stick[1], z[1], ACT.Exp).then_inc(sb_w_done, 1)
                if kind == "sb":
                    split_sb(k, 1, p + 2)
                if kind == "mla":
                    split_kv(k, 6)
                if last:
                    split_rotary(k, 0, 11, 6, 2, HD)
                act.wait_ge(sb_pv_done, p * 2 + 1)
                act.activation(h[0:HD, bass.ds(p, 1), :], ps[0:HD, 7:8, :], ACT.Copy).then_inc(sb_oA_copied, 1)

            def latent_hi(ct0, ct1):
                for ct in range(ct0, ct1):
                    act.wait_ge(lat_scaled, ct + 1)
                    act.activation(xT_hi[:, ct, :], latent[ct], ACT.Copy).then_inc(lat_hi_done, 1)

            def mla_query_copy(n, a):
                act.wait_ge(mq_done, n * 2 + (a + 1))
                act.activation(mq[a][0:HD, :], ps[0:HD, 6 + a, :], ACT.Copy).then_inc(mq_nope_copied, 1)

            def mla_key_copy(n):
                act.wait_ge(mk_done, n + 1)
                for a in range(2):
                    act.activation(mk[a][0:HD, :], ps[HD * a:HD * a + HD, 6, :], ACT.Copy).then_inc(mk_copied, 1)

            def mla_value_copy(n, bank=7):
                act.wait_ge(mv_done, n + 1)
                act.activation(mla_vT, ps[:, bank, :], ACT.Copy).then_inc(mvT_copied, 1)

            def mla_exp(p, a, t):
                act.wait_ge(max_ready, p * 8 + (4 * a + t + 1))
                if a == 1:
                    act.wait_ge(p_turned, p * 8 + (t + 1))
                keys = P * (t + 1)
                act.activation(prob[t][:, 0:keys], ps[:, t, 0:keys], ACT.Exp, bias=neg_max[:, t:t + 1],
                               accum_out=p_sum[:, t:t + 1]).then_inc(exp_done, 1)

            def mla_turned_copy(p, a, t):
                n = 4 * a + t
                act.wait_ge(p_turned, p * 8 + (n + 1))
                act.activation(pT[a][:, 0:t + 1, t * P:(t + 1) * P],
                               ps[:, 4 + n % 2, 0:P * (t + 1)].rearrange("p (k n) -> p k n", n=P),
                               ACT.Copy).then_inc(pT_copied, 1)

            def mla_pair(k, p, kind):
                more = kind != "last"
                for t in range(TT):
                    mla_exp(p, 0, t)
                if more:
                    mla_query_copy(p + 1, 0)
                mla_turned_copy(p, 0, 0)
                mla_turned_copy(p, 0, 1)
                mla_exp(p, 1, 0)
                mla_exp(p, 1, 1)
                mla_turned_copy(p, 0, 2)
                mla_turned_copy(p, 0, 3)
                mla_exp(p, 1, 2)
                mla_exp(p, 1, 3)
                if more:
                    mla_query_copy(p + 1, 1)
                mla_turned_copy(p, 1, 0)
                mla_turned_copy(p, 1, 1)
                if more:
                    mla_key_copy(p + 1)
                mla_turned_copy(p, 1, 2)
                mla_turned_copy(p, 1, 3)
                if kind == "mla":
                    split_rotary(k, 0, p + 12, 6, 2, HD)
                if kind == "out":
                    split_w(k, 0, 10, dmas=before(SLOT_DMAS, k, 0) + 15)
                    act.wait_ge(sb_oA_copied, HEAD_PAIRS + 1)
                    act.wait_ge(sb_oB_copied, HEAD_PAIRS + 1)
                    split_left(0, 0)
                if kind == "last":
                    split_w(k, 2, 1)
                act.wait_ge(mla_pv_done, p * 2 + 1)
                act.activation(h[0:HD, bass.ds(p + 4, 1), :], ps[0:HD, 6:7, :], ACT.Copy).then_inc(mla_oA_copied, 1)
                if more:
                    mla_value_copy(p + 1)
                if kind == "mla":
                    split_kv(k, p + 8)
                if kind == "out":
                    split_w(k, 1, 10)
                    split_left(1, 2)

            act.sem_inc(silu_done, 2)
            act.sem_inc(c_copied, 2)
            act.sem_inc(sb_oA_copied, 1)
            turn_hi(0, 0)
            turn_hi(0, 1)
            split_w(0, 0, 0)
            turn_hi(0, 2)
            split_w(0, 1, 0)
            turn_hi(0, 3)
            act.wait_ge(consts_in, 96)
            act.activation(ident_r[:], ident, ACT.Copy).then_inc(masks_ready, 1)
            act.activation(tri_r[:, 0:P], cst[:, C_NEG_ONES:C_NEG_ONES + P], ACT.Copy).then_inc(masks_ready, 1)
            act.activation(tri_r[:, P:], mask_source[:, 0:P], ACT.Copy).then_inc(masks_ready, 1)
            act.activation(not_past_r[:], mask_source[:, P:], ACT.Copy).then_inc(masks_ready, 1)

            for k, (kind, layer, idx) in enumerate(stages):
                d0 = before(DOWN_USED, k)
                if kind == "ffn":
                    p0 = FT * ffns_before(k)

                    def silu_pair(i):
                        for c in range(2):
                            act.wait_ge(gate_done, i * 2 + (p0 + 1 + c))
                            act.wait_ge(h_done, i * 2 + (p0 + 1 + c))
                            act.activation(gs[:, c, :], ps[:, c, :], ACT.Silu).then_inc(silu_done, 1)

                    def split_next(i):
                        act.wait_ge(gate_done, i * 2 + (p0 + 2))
                        split_w(k, 0, i + 1)
                        act.wait_ge(up_done, i * 2 + (p0 + 2))
                        split_w(k, 1, i + 1)

                    with act.Fori(0, PAIRS - 1) as i:
                        silu_pair(i)
                        split_next(i)
                    if k > 0:
                        act.wait_ge(y_done, 8 * k)
                    act.wait_ge(h_done, p0 + 4 + 2)
                    for s in range(2):
                        split_left(s, 2 * s)
                    silu_pair(PAIRS - 1)
                    split_next(PAIRS - 1)
                    split_w(k, 2, 0)
                    act.wait_ge(h_done, p0 + FT + 2)
                    split_left(2, FT - 2)
                    with act.Fori(1, (DOWN_UNITS - 1) // 2) as i:
                        for s in range(2):
                            act.wait_ge(down_used, i * 2 + (d0 + s - 1))
                            split_left(s, i * 4 + 2 * s)
                            split_w(k, s, i + PAIRS)
                if kind == "conv":
                    split_w(k, 2, 0)

                    def conv_pair(i, last):
                        for c in range(2):
                            act.wait_ge(conv_c_done, i * 2 + (1 + c))
                            act.wait_ge(u_done, i * 2 + (1 + c))
                            act.activation(gs[:, c, :], ps[:, c, :], ACT.Copy).then_inc(c_copied, 1)
                        for s, done in enumerate((conv_c_done, conv_h_done, conv_b_done)):
                            if last:
                                act.wait_ge(conv_out_done, 2 * s + 4)
                                split_left(s, 2 * s)
                            act.wait_ge(done, i * 2 + 2)
                            split_w(k, s, i + 1)

                    with act.Fori(0, KT // 2 - 1) as i:
                        conv_pair(i, False)
                    conv_pair(KT // 2 - 1, True)
                    act.wait_ge(conv_out_done, KT + 2)
                    act.wait_ge(down_used, d0 + 1)
                    split_left(0, 6)
                    split_w(k, 0, 5)
                if kind == "attn":
                    latent_tiles(k)
                    sb_query_hi(0)
                    sb_key_hi(0)
                    split_sb(k, 0, 1)
                    for n, (width, scale) in enumerate(((Q_RANK, MLA_SCALE), (KV_RANK, 1.0))):
                        act.wait_ge(sum_done, n + 1)
                        act.activation(sq_sum[n], ps[:, 1 + n, :], ACT.Sqrt, scale=-1.0 / (width * scale ** 2),
                                       bias=rms_eps[:, n:n + 1]).then_inc(mean_root, 1)
                        if n == 0:
                            act.wait_ge(sq_added, KT)
                            sb_value_copy(0)
                    split_sb(k, 1, 1)
                    act.preload_act_table_set("natural_log_exp_and_others")
                    with act.Fori(0, HEAD_PAIRS - 2) as p:
                        sb_pair(k, p, "sb")
                    sb_pair(k, HEAD_PAIRS - 2, "mla")
                    latent_hi(4, KT)
                    sb_pair(k, HEAD_PAIRS - 1, "last")
                    act.wait_ge(k_rope_placed, 2)
                    mla_value_copy(0, 5)
                    split_kv(k, 7)
                    with act.Fori(0, HEAD_PAIRS - 2) as p:
                        mla_pair(k, p, "mla")
                    mla_pair(k, HEAD_PAIRS - 2, "out")
                    mla_pair(k, HEAD_PAIRS - 1, "last")
                    act.wait_ge(mla_oA_copied, HEAD_PAIRS)
                    act.wait_ge(mla_oB_copied, HEAD_PAIRS + 1)
                    split_left(2, 4)
                    act.wait_ge(down_used, d0 + 1)
                    split_w(k, 0, 11, dmas=before(SLOT_DMAS, k, 0) + 16)
                    split_left(0, 6)
                close_stage(k)

        @block.vector
        def _(dve):
            def split_w(k, s, n, width=UNIT):
                dve.wait_ge(w_hi_done[s], n + (before(SLOT_UNITS, k, s) + 1))
                dve.tensor_tensor(w_lo[s][:, 0:width], raw[s][:, 0:width], w_hi[s][:, 0:width],
                                  ALU.subtract).then_inc(w_lo_done[s], 1)

            def split_left(k, s, n, f):
                dve.wait_ge(left_hi_done[s], n + (before(LEFT_UNITS, k, s) + 1))
                dve.tensor_tensor(left_lo[s][:], h[:, bass.ds(f, 2), :], left_hi[s][:],
                                  ALU.subtract).then_inc(left_lo_done[s], 1)

            def turn_lo(m, t):
                for half in range(2):
                    dve.wait_ge(xT_hi_done, 8 * m + 2 * t + half + 1)
                    k4 = slice(4 * half, 4 * half + 4)
                    dve.tensor_tensor(xT_lo[:, k4, t * P:(t + 1) * P],
                                      ps[:, 2 * t + half, :].rearrange("p (k n) -> p k n", k=4),
                                      xT_hi[:, k4, t * P:(t + 1) * P], ALU.subtract).then_inc(xT_ready, 1)

            def layer_norm(k, t, scale):
                b = 6 * (TT * k + t)
                dve.wait_ge(res_ready, TT * k + t + 1)
                for half in range(2):
                    dve.wait_ge(y_done, 8 * k + 2 * t + half + 1)
                    part = xn[:, t, half * HALF:(half + 1) * HALF]
                    dve.scalar_tensor_tensor(part, ps[:, 2 * t + half, :], scale, part,
                                             ALU.mult, ALU.add).then_inc(ln_step, 1)
                for half in range(2):
                    dve.wait_ge(ln_step, b + half + 1)
                    dve.bn_stats(stats[:, half, :], xn[:, t, half * HALF:(half + 1) * HALF]).then_inc(ln_step, 1)
                dve.wait_ge(ln_step, b + 4)
                dve.bn_aggr(mean_var[:], stats[:].rearrange("p a b -> p (a b)")).then_inc(ln_step, 1)
                dve.wait_ge(ln_step, b + 5)
                dve.tensor_scalar(veps[:], mean_var[:, 1:2], LN_EPS, None, ALU.add).then_inc(var_ready, 1)
                if t == 0:
                    dve.wait_ge(gb_full, 32 * (k + 1))
                dve.scalar_tensor_tensor(xn[:, t, :], xn[:, t, :], mean_var[:, 0:1], gb[:, 0, :],
                                         ALU.subtract, ALU.mult).then_inc(ln_step, 1)
                dve.wait_ge(ln_step, b + 6)
                dve.wait_ge(rstd_ready, TT * k + t + 1)
                parts = 2 if (k, t) == (n_stages - 1, TT - 1) else 1
                for n in range(parts):
                    cut = slice(n * D // parts, (n + 1) * D // parts)
                    dve.scalar_tensor_tensor(xn[:, t, cut], xn[:, t, cut], rstd[:, t:t + 1], gb[:, 1, cut],
                                             ALU.mult, ALU.add).then_inc(x_done, 1)

            def rotary_lo(k, s, n, kts, heads, lead):
                half = ROPE // 2
                dve.wait_ge(w_hi_done[s], n + (before(SLOT_UNITS, k, s) + 1))
                hi, lo = (w[:, 0:kts * heads * P].rearrange("p (k a n) -> p k a n", k=kts, a=heads)
                          for w in (w_hi[s], w_lo[s]))
                r = raw[s][:, 0:kts * heads * (lead + ROPE)].rearrange("p (k a n) -> p k a n", k=kts, a=heads)
                for dst, src in ((slice(HD - lead, HD + ROPE), slice(0, lead + ROPE)),
                                 (slice(HD + ROPE, HD + ROPE + half), slice(lead + half, lead + ROPE)),
                                 (slice(HD + ROPE + half, P), slice(lead, lead + half))):
                    last = dve.tensor_tensor(lo[:, :, :, dst], r[:, :, :, src], hi[:, :, :, dst], ALU.subtract)
                last.then_inc(w_lo_done[s], 1)

            def kv_lo(k, n):
                dve.wait_ge(w_hi_done[1], n + (before(SLOT_UNITS, k, 1) + 1))
                for part in range(2):
                    last = dve.tensor_tensor(kv_view(w_lo[1], part), kv_raw(part), kv_view(w_hi[1], part), ALU.subtract)
                last.then_inc(w_lo_done[1], 1)

            def rotate(dst, bank, base, step, done):
                dve.tensor_tensor(dst[HD:HD + ROPE, :], ps[HD:HD + ROPE, bank, :], rope_sb[HD:HD + ROPE, :],
                                  ALU.mult).then_inc(step, 1)
                dve.tensor_tensor(rope_tmp[HD:HD + ROPE, :], ps[HD + ROPE:P, bank, :], rope_sb[HD + ROPE:P, :],
                                  ALU.mult).then_inc(step, 1)
                dve.wait_ge(step, base + 2)
                dve.tensor_tensor(dst[HD:HD + ROPE, :], dst[HD:HD + ROPE, :], rope_tmp[HD:HD + ROPE, :],
                                  ALU.add).then_inc(done, 1)

            def sb_query_lo(n):
                dve.wait_ge(sbq_hi_done, n + 1)
                dve.scalar_tensor_tensor(sbq[1], ps[:, 6, :], HD ** -0.5, sbq[0],
                                         ALU.mult, ALU.subtract).then_inc(sbq_ready, 1)

            def sb_key_lo(n):
                dve.wait_ge(sbk_hi_done, n + 1)
                dve.tensor_tensor(sbk[1], ps[:, 7, :], sbk[0], ALU.subtract).then_inc(sbk_ready, 1)

            def sb_value_copy(n):
                dve.wait_ge(sb_v_turned, n + 1)
                dve.tensor_copy(sb_v, ps[:, 5, :].rearrange("p (k n) -> p k n", n=P)).then_inc(sb_v_ready, 1)

            def latent_norm(n):
                dve.wait_ge(mean_root, n + 1)
                dve.reciprocal(sq_sum[n], sq_sum[n]).then_inc(rms_ready, 1)

            def sb_pair(k, p, kind):
                last = kind == "last"
                for a in range(2):
                    dve.wait_ge(log_ready, p * 2 + (a + 1))
                    dve.scalar_tensor_tensor(stick[a], z[a], 0.0, stick[a], ALU.max, ALU.add).then_inc(keep_step, 1)
                    dve.wait_ge(keep_step, p * 4 + (2 * a + 1))
                    past = cst[:, C_PAST:C_PAST + P]
                    last_tile = stick[a][:, Z_AT[3]:Z_AT[3] + P]
                    dve.tensor_tensor(last_tile, last_tile, past, ALU.mult).then_inc(keep_step, 1)
                    for i in range(3):
                        diag = stick[a][:, Z_AT[i]:Z_AT[i] + P]
                        mm = dve.tensor_tensor(diag, diag, past, ALU.mult)
                    mm.then_inc(keep_ready, 1)
                for a in range(2):
                    dve.wait_ge(stick_hi_done, p * 2 + (a + 1))
                    w = (w_hi, w_lo)[a]
                    dve.tensor_tensor(w[1][:, KT * P:2 * KT * P], stick[a][:, 0:KT * P], stick_hi[a][:, 0:KT * P],
                                      ALU.subtract)
                    dve.tensor_tensor(stick_lo(a, 2), stick[a][:, KT * P:Z_W], stick_hi[a][:, KT * P:Z_W],
                                      ALU.subtract).then_inc(stick_ready, 1)
                    if last:
                        mla_query_rope(0, a)
                    else:
                        (sb_query_lo, sb_key_lo)[a](p + 1)
                if kind == "sb":
                    split_w(k, 0, p + 4)
                    split_w(k, 1, p + 4, width=KT * P)
                if kind == "mla":
                    rotary_lo(k, 0, 6, 6, 2, HD)
                    latent_lo(0, 4)
                    kv_lo(k, 6)
                if last:
                    rotary_lo(k, 0, 7, 6, 2, HD)
                dve.wait_ge(sb_pv_done, p * 2 + 2)
                dve.tensor_copy(h[HD:P, bass.ds(p, 1), :], ps[HD:P, 6:7, :]).then_inc(sb_oB_copied, 1)
                if not last:
                    sb_value_copy(p + 1)

            def latent_scale():
                for ct in range(KT):
                    n = 0 if ct < 6 else 1
                    dve.wait_ge(rms_ready, n + 1)
                    g = cols[:, ROWS_QG + ct:ROWS_QG + ct + 1]
                    dve.scalar_tensor_tensor(latent[ct], latent[ct], g, sq_sum[n], ALU.mult, ALU.mult).then_inc(lat_scaled, 1)

            def latent_lo(ct0, ct1):
                for ct in range(ct0, ct1):
                    dve.wait_ge(lat_hi_done, ct + 1)
                    dve.tensor_tensor(xT_lo[:, ct, :], latent[ct], xT_hi[:, ct, :], ALU.subtract).then_inc(lat_ready, 1)

            def mla_query_rope(n, a):
                dve.wait_ge(mq_done, n * 2 + (a + 1))
                dve.wait_ge(mq_nope_copied, n * 2 + (a + 1))
                dve.wait_ge(*((kr_step, 3) if isinstance(n, int) and n + a == 0 else (mq_rope_ready, n * 2 + a)))
                rotate(mq[a], 6 + a, n * 4 + 2 * a, mq_step, mq_rope_ready)

            def mla_max(p, a, t):
                n = 4 * a + t
                dve.wait_ge(s_done, p * 8 + (n + 1))
                diag = ps[:, t, t * P:(t + 1) * P]
                dve.tensor_tensor(diag, diag, cst[:, C_CAUSAL:C_CAUSAL + P], ALU.add).then_inc(max_step, 1)
                dve.wait_ge(max_step, p * 8 + (n + 1))
                dve.tensor_reduce(neg_max[:, t:t + 1], ps[:, t, 0:P * (t + 1)], AX.X, ALU.max,
                                  negate=True).then_inc(max_ready, 1)

            def mla_norm(p, a, t):
                n = 4 * a + t
                dve.wait_ge(exp_done, p * 8 + (n + 1))
                dve.reciprocal(p_sum[:, t:t + 1], p_sum[:, t:t + 1]).then_inc(norm_step, 1)
                dve.wait_ge(norm_step, p * 8 + (n + 1))
                rows_t = prob[t][:, 0:P * (t + 1)]
                dve.tensor_scalar(rows_t, rows_t, p_sum[:, t:t + 1], None, ALU.mult).then_inc(p_ready, 1)

            def mla_value_copy(n):
                dve.wait_ge(mv_turned, n + 1)
                dve.tensor_copy(mv, ps[:, 3, :].rearrange("p (k n) -> p k n", n=P)).then_inc(mv_ready, 1)

            def mla_pair(k, p, kind):
                more = kind != "last"
                mla_max(p, 0, 0)
                mla_max(p, 0, 1)
                mla_norm(p, 0, 0)
                mla_max(p, 0, 2)
                mla_norm(p, 0, 1)
                mla_max(p, 0, 3)
                mla_norm(p, 0, 2)
                mla_norm(p, 0, 3)
                if more:
                    mla_query_rope(p + 1, 0)
                mla_max(p, 1, 0)
                mla_max(p, 1, 1)
                mla_norm(p, 1, 0)
                mla_norm(p, 1, 1)
                mla_max(p, 1, 2)
                mla_max(p, 1, 3)
                mla_norm(p, 1, 2)
                mla_norm(p, 1, 3)
                if more:
                    mla_query_rope(p + 1, 1)
                if kind == "mla":
                    rotary_lo(k, 0, p + 8, 6, 2, HD)
                if kind == "out":
                    split_w(k, 0, 10)
                    split_left(k, 0, 0, 0)
                if kind == "last":
                    split_w(k, 2, 1)
                dve.wait_ge(mla_pv_done, p * 2 + 2)
                bank = 6 if more else 4
                dve.tensor_copy(h[HD:P, bass.ds(p + 4, 1), :], ps[HD:P, bank:bank + 1, :]).then_inc(mla_oB_copied, 1)
                if more:
                    mla_value_copy(p + 1)
                if kind == "mla":
                    kv_lo(k, p + 8)
                if kind == "out":
                    split_w(k, 1, 10)
                    split_left(k, 1, 0, 2)

            def close_stage(k, scale):
                more = k + 1 < n_stages
                layer_norm(k, 0, scale)
                layer_norm(k, 1, scale)
                if more:
                    turn_lo(k + 1, 0)
                layer_norm(k, 2, scale)
                if more:
                    turn_lo(k + 1, 1)
                layer_norm(k, 3, scale)
                if more:
                    turn_lo(k + 1, 2)
                    turn_lo(k + 1, 3)

            dve.sem_inc(h_done, 2)
            dve.sem_inc(u_done, 2)
            dve.sem_inc(conv_out_done, 2)
            dve.sem_inc(sb_oB_copied, 1)
            dve.sem_inc(mla_oB_copied, 1)
            turn_lo(0, 0)
            turn_lo(0, 1)
            split_w(0, 0, 0)
            turn_lo(0, 2)
            split_w(0, 1, 0)
            turn_lo(0, 3)

            for k, (kind, layer, idx) in enumerate(stages):
                if kind == "ffn":
                    p0 = FT * ffns_before(k)

                    def gated_pair(i):
                        for c in range(2):
                            dve.wait_ge(silu_done, i * 2 + (p0 + 3 + c))
                            dve.wait_ge(up_done, i * 2 + (p0 + 1 + c))
                            dve.tensor_tensor(h[:, bass.ds(i * 2 + c, 1), :], gs[:, c:c + 1, :], ps[:, 2 + c:3 + c, :],
                                              ALU.mult).then_inc(h_done, 1)

                    with dve.Fori(0, PAIRS - 1) as i:
                        split_w(k, 0, i + 1)
                        gated_pair(i)
                        split_w(k, 1, i + 1)
                    if k == 0:
                        dve.wait_ge(rows_turned, 1)
                        dve.tensor_copy(cols[:], ps[:, 7, 0:N_ROWS]).then_inc(cols_ready, 1)
                    for s in range(2):
                        split_left(k, s, 0, 2 * s)
                    split_w(k, 0, PAIRS)
                    gated_pair(PAIRS - 1)
                    split_w(k, 1, PAIRS)
                    split_w(k, 2, 0)
                    split_left(k, 2, 0, FT - 2)
                    with dve.Fori(1, (DOWN_UNITS - 1) // 2) as i:
                        for s in range(2):
                            split_left(k, s, i, i * 4 + 2 * s)
                            split_w(k, s, i + PAIRS)
                    close_stage(k, 0.5)
                if kind == "conv":
                    for c in range(2):
                        dve.memset(conv_u[c][:, 0:U_PAD], 0.0).then_inc(u_zeroed, 1)
                    dve.wait_ge(u_zeroed, 2)
                    split_w(k, 2, 0)

                    def conv_tile(i, c):
                        dve.wait_ge(u_done, i * 2 + (3 + c))
                        dve.tensor_scalar(conv_acc[c], conv_u[c][:, 2:2 + S], taps[:, 2, c:c + 1], None,
                                          ALU.mult).then_inc(conv_step, 1)
                        for n, tap in enumerate((1, 0)):
                            dve.wait_ge(conv_step, i * 6 + (3 * c + n + 1))
                            dve.scalar_tensor_tensor(conv_acc[c], conv_u[c][:, tap:tap + S], taps[:, tap, c:c + 1],
                                                     conv_acc[c], ALU.mult, ALU.add).then_inc(conv_step, 1)

                    def conv_pair(i, last):
                        dve.tensor_copy(taps[:], cols[:, ROWS_TAPS:ROWS_QG].rearrange("p (k c) -> p k c", k=3)
                                        [:, :, bass.ds(i * 2, 2)]).then_inc(taps_set, 1)
                        if last:
                            split_left(k, 0, 0, 0)
                        split_w(k, 0, i + 1)
                        dve.wait_ge(taps_set, i + 1)
                        for c in range(2):
                            dve.wait_ge(c_copied, i * 2 + (3 + c))
                            dve.wait_ge(conv_h_done, i * 2 + (1 + c))
                            dve.tensor_tensor(conv_u[c][:, U_PAD:U_PAD + S], gs[:, c, :], ps[:, 2 + c, :],
                                              ALU.mult).then_inc(u_done, 1)
                            conv_tile(i, c)
                        if last:
                            split_left(k, 1, 0, 2)
                        split_w(k, 1, i + 1)
                        for c in range(2):
                            dve.wait_ge(conv_step, i * 6 + (3 * c + 3))
                            dve.wait_ge(conv_b_done, i * 2 + (1 + c))
                            dve.tensor_tensor(h[:, bass.ds(i * 2 + c, 1), :],
                                              conv_acc[c].rearrange("p (a n) -> p a n", a=1),
                                              ps[:, 4 + c:5 + c, :], ALU.mult).then_inc(conv_out_done, 1)
                        if last:
                            split_left(k, 2, 0, 4)
                        split_w(k, 2, i + 1)

                    with dve.Fori(0, KT // 2 - 1) as i:
                        conv_pair(i, False)
                    conv_pair(KT // 2 - 1, True)
                    split_left(k, 0, 1, 6)
                    split_w(k, 0, 5)
                    close_stage(k, 1.0)
                if kind == "attn":
                    split_w(k, 0, 1)
                    rotary_lo(k, 2, 0, KT, 1, 0)
                    split_w(k, 1, 1)
                    dve.wait_ge(kr_done, 1)
                    rotate(k_rope, 4, 0, kr_step, kr_step)
                    split_w(k, 0, 2)
                    split_w(k, 1, 2, width=KT * P)
                    sb_query_lo(0)
                    sb_key_lo(0)
                    split_w(k, 0, 3)
                    latent_norm(0)
                    sb_value_copy(0)
                    split_w(k, 1, 3, width=KT * P)
                    latent_norm(1)
                    with dve.Fori(0, HEAD_PAIRS - 2) as p:
                        sb_pair(k, p, "sb")
                    latent_scale()
                    sb_pair(k, HEAD_PAIRS - 2, "mla")
                    dve.wait_ge(lat_scaled, KT)
                    for a in range(2):
                        dve.tensor_copy(mk[a][HD:HD + ROPE, :], k_rope[HD:HD + ROPE, :]).then_inc(k_rope_placed, 1)
                    latent_lo(4, KT)
                    sb_pair(k, HEAD_PAIRS - 1, "last")
                    mla_value_copy(0)
                    kv_lo(k, 7)
                    with dve.Fori(0, HEAD_PAIRS - 2) as p:
                        mla_pair(k, p, "mla")
                    mla_pair(k, HEAD_PAIRS - 2, "out")
                    mla_pair(k, HEAD_PAIRS - 1, "last")
                    split_left(k, 2, 0, 4)
                    split_w(k, 0, 11)
                    split_left(k, 0, 1, 6)
                    close_stage(k, 1.0)

        @block.gpsimd
        def _(pool):
            pool.memset(half_neg[:], -0.5).then_inc(exp_ready, 1)
            for n, scale in enumerate((MLA_SCALE, 1.0)):
                pool.memset(rms_eps[:, n:n + 1], RMS_EPS / scale ** 2).then_inc(exp_ready, 1)
            pool.wait_ge(exp_ready, 3)
            for k, (kind, layer, idx) in enumerate(stages):
                if k > 0:
                    pool.wait_ge(x_done, TT * k)
                pool.dma_start(gb[:, 0, :], ln_g[layer, idx].partition_broadcast(P)).then_inc(gb_full, 16)
                pool.dma_start(gb[:, 1, :], ln_b[layer, idx].partition_broadcast(P)).then_inc(gb_full, 16)
                for t in range(TT):
                    pool.wait_ge(turned, 8 * k + 2 * t + 2)
                    pool.tensor_scalar(xn[:, t, :], xn[:, t, :], ALPHA, None, ALU.mult).then_inc(res_ready, 1)
                if kind == "attn":
                    pool.wait_ge(w_lo_done[2], before(SLOT_UNITS, k, 2))
                    for n in range(2):
                        pool.memset(sq_sum[n], 0.0).then_inc(sums_zeroed, 1)
                    for ct in range(KT):
                        n = 0 if ct < 6 else 1
                        pool.wait_ge(lat_squared, ct + 1)
                        if ct in (0, 6):
                            pool.wait_ge(sums_zeroed, 2)
                        else:
                            pool.wait_ge(sq_added, ct)
                        pool.tensor_tensor(sq_sum[n], sq_sum[n], gs[:, ct % 2, :], ALU.add).then_inc(sq_added, 1)
                for t in range(TT):
                    pool.wait_ge(var_ready, TT * k + t + 1)
                    pool.tensor_tensor(rstd[:, t:t + 1], veps[:], half_neg[:], ALU.pow).then_inc(rstd_ready, 1)
                    if t >= 2 and k + 1 < n_stages:
                        s = t - 2
                        pool.wait_ge(w_hi_done[s], before(SLOT_UNITS, k + 1, s) + 1)
                        pool.tensor_tensor(w_lo[s][:], raw[s][:], w_hi[s][:], ALU.subtract).then_inc(w_lo_done[s], 1)


def shape_constants():
    c = np.zeros((P, C_COLS), np.float32)
    row, col = np.arange(P)[:, None], np.arange(P)[None, :]
    c[:, C_IDENT:C_IDENT + P] = row == col
    c[:, C_NEG_ONES:C_NEG_ONES + P] = -1.0
    c[:, C_NEG_TRI:C_NEG_TRI + P] = -1.0 * (row >= col)
    c[:, C_PAST:C_PAST + P] = row < col
    c[:, C_NOT_PAST:C_NOT_PAST + P] = np.where(row < col, 0.0, -1e30)
    c[:, C_CAUSAL:C_CAUSAL + P] = np.where(col <= row, 0.0, -1e30)
    half = ROPE // 2
    inv = np.float32(10000.0) ** (-np.arange(0, ROPE, 2, dtype=np.float32) / np.float32(ROPE))
    ang = (np.arange(S, dtype=np.float32)[None, :] * inv.astype(np.float32)[:, None]).astype(np.float32)
    r = np.zeros((2 * ROPE, S), np.float32)
    r[0:half] = r[half:ROPE] = np.cos(ang)
    r[ROPE:ROPE + half] = -np.sin(ang)
    r[ROPE + half:] = np.sin(ang)
    return c, r


INPUTS = ("x", "ln_g", "ln_b", "ffn_w_gate", "ffn_w_up", "ffn_w_down", "mix_w_in", "mla_q_norm_g", "mla_w_uq",
          "mla_kv_norm_g", "mla_w_ukv", "mix_w_out", "conv_w_in", "conv_w", "conv_w_out")


def kernel(**inputs):
    from concourse import bacc
    from concourse.bass_utils import run_bass_kernel_spmd

    nc = bacc.Bacc("TRN2", target_bir_lowering=False, num_devices=1)
    arrays = {name: np.ascontiguousarray(inputs[name]) for name in INPUTS}
    arrays["shape_consts"], arrays["rope_tables"] = shape_constants()
    args = [nc.dram_tensor(n, a.shape, mybir.dt.from_np(a.dtype), kind="ExternalInput").ap() for n, a in arrays.items()]
    args.append(nc.dram_tensor("trunk_out", (1, S, D), F32, kind="ExternalOutput").ap())
    build_trunk(nc, *args)
    result = run_bass_kernel_spmd(nc, [arrays], core_ids=[0])
    return result.results[0]["trunk_out"]
```
